# Optimizing a Trainium2 kernel written in Bass

```python
import jax
import jax.numpy as jnp
from jax import lax
import numpy as np

D_MODEL = 1024
BATCH = 1
SEQ = 512
DEPTH = 2

CTX_LEN = 256
GRID_W = 64
EPS = 1e-6
ROPE_THETA = 10000.0
Q_BLOCK = 128

D_MIX = D_MODEL
N_MIXERS = 4
GROUP_W = D_MIX // N_MIXERS

A_HEADS = 4
A_HEAD_DIM = GROUP_W // A_HEADS
CHUNK = 128

CONV_W = 3

C_HEADS = 4
C_KV_HEADS = 2
C_GROUP = C_HEADS // C_KV_HEADS
C_HEAD_DIM = GROUP_W // C_HEADS
C_SCALE = C_HEAD_DIM ** -0.5

D_HEADS = 4
D_V = GROUP_W // D_HEADS
D_NOPE = D_V
D_ROPE = D_NOPE // 2
D_Q_LORA = D_MIX // 4
D_KV_LORA = D_MIX // 8
D_SCALE = (D_NOPE + D_ROPE) ** -0.5

IN_SPLITS = (GROUP_W, GROUP_W,
             GROUP_W, GROUP_W, GROUP_W,
             C_HEADS * C_HEAD_DIM, C_KV_HEADS * C_HEAD_DIM, C_KV_HEADS * C_HEAD_DIM,
             D_Q_LORA, D_KV_LORA, D_ROPE)
IN_COLS = sum(IN_SPLITS)
IN_SPLIT_IDX = tuple(int(i) for i in np.cumsum(IN_SPLITS)[:-1])

N_GROUPS = 4
EXPERTS_PER_GROUP = 4
N_EXPERTS = N_GROUPS * EXPERTS_PER_GROUP
TOP_K = 2
D_EXPERT = D_MODEL // 4

kernel_name = 'hybrid_head_group_moe_dit'

def _rms_norm(x, gain):
    xf = x.astype(jnp.float32)
    y = xf * lax.rsqrt(jnp.mean(xf * xf, axis=-1, keepdims=True) + EPS)
    return (y * gain.astype(jnp.float32)).astype(x.dtype)

def _modulate(h, shift, scale):
    return h * (1 + scale) + shift

def _axial_rope(rows, rot_dim):
    row = jnp.repeat(jnp.arange(rows, dtype=jnp.float32), GRID_W)
    col = jnp.tile(jnp.arange(GRID_W, dtype=jnp.float32), rows)
    n_freq = rot_dim // 4
    inv_freq = ROPE_THETA ** (-jnp.arange(n_freq, dtype=jnp.float32) / n_freq)
    ang = jnp.concatenate([row[:, None] * inv_freq, col[:, None] * inv_freq], axis=-1)
    return jnp.cos(ang), jnp.sin(ang)

def _apply_rope(x, cos, sin):
    xp = x.astype(jnp.float32).reshape(*x.shape[:-1], x.shape[-1] // 2, 2)
    x0, x1 = xp[..., 0], xp[..., 1]
    cs, sn = cos[None, :, None, :], sin[None, :, None, :]
    out = jnp.stack([x0 * cs - x1 * sn, x0 * sn + x1 * cs], axis=-1)
    return out.reshape(x.shape).astype(x.dtype)

def _attention(q, k, v, scale):
    s = jnp.einsum('bqhgd,bkhd->bhgqk', q, k).astype(jnp.float32) * scale
    p = jax.nn.softmax(s, axis=-1).astype(v.dtype)
    return jnp.einsum('bhgqk,bkhd->bqhgd', p, v)

def _blocked_attention(q, k, v, scale):
    b, n = q.shape[:2]
    qb = jnp.moveaxis(q.reshape(b, n // Q_BLOCK, Q_BLOCK, *q.shape[2:]), 1, 0)
    ob = lax.map(lambda qblk: _attention(qblk, k, v, scale), qb)
    return jnp.moveaxis(ob, 0, 1).reshape(b, n, *ob.shape[3:])

def _chunk_sgu(u, v, v_gain, w_s, b_s):
    b, n, _ = u.shape
    u = jax.nn.gelu(u)
    v = _rms_norm(jax.nn.gelu(v).reshape(b, n // CHUNK, CHUNK, A_HEADS, A_HEAD_DIM),
                  v_gain.reshape(A_HEADS, A_HEAD_DIM))
    mixed = jnp.einsum('hij,bcjhd->bcihd', w_s, v) + b_s.T[:, :, None]
    return u * mixed.reshape(b, n, GROUP_W)

def _short_conv(bg, cg, xin, w_conv):
    z = cg * xin
    z = lax.conv_general_dilated(z, w_conv[:, None, :], window_strides=(1,),
                                 padding=((CONV_W // 2, CONV_W // 2),),
                                 dimension_numbers=('NWC', 'WIO', 'NWC'),
                                 feature_group_count=GROUP_W)
    return bg * z

def _gqa_qkv(q, k, v, q_gain, k_gain, rope):
    b, n = q.shape[:2]
    q = _rms_norm(q.reshape(b, n, C_HEADS, C_HEAD_DIM), q_gain)
    k = _rms_norm(k.reshape(b, n, C_KV_HEADS, C_HEAD_DIM), k_gain)
    v = v.reshape(b, n, C_KV_HEADS, C_HEAD_DIM)
    if rope is not None:
        q = _apply_rope(q, *rope)
        k = _apply_rope(k, *rope)
    return q.reshape(b, n, C_KV_HEADS, C_GROUP, C_HEAD_DIM), k, v

def _mla_qkv(cq, ckv, kr, qa_gain, w_qb, kva_gain, w_kvb, q_gain, k_gain, rope):
    b, n = cq.shape[:2]
    q = (_rms_norm(cq, qa_gain) @ w_qb).reshape(b, n, D_HEADS, D_NOPE + D_ROPE)
    kv = (_rms_norm(ckv, kva_gain) @ w_kvb).reshape(b, n, D_HEADS, D_NOPE + D_V)
    q_nope = _rms_norm(q[..., :D_NOPE], q_gain[:D_NOPE])
    q_rope = _rms_norm(q[..., D_NOPE:], q_gain[D_NOPE:])
    k_nope = _rms_norm(kv[..., :D_NOPE], k_gain[:D_NOPE])
    k_rope = _rms_norm(kr[:, :, None, :], k_gain[D_NOPE:])
    if rope is not None:
        q_rope = _apply_rope(q_rope, *rope)
        k_rope = _apply_rope(k_rope, *rope)
    q = jnp.concatenate([q_nope, q_rope], axis=-1)[:, :, :, None, :]
    k = jnp.concatenate([k_nope, jnp.broadcast_to(k_rope, (b, n, D_HEADS, D_ROPE))], axis=-1)
    return q, k, kv[..., D_NOPE:]

def _merge_groups(ys, g_group_out, w_out):
    y = jnp.concatenate([yy.reshape(*yy.shape[:2], GROUP_W) for yy in ys], axis=-1)
    b, n = y.shape[:2]
    y = _rms_norm(y.reshape(b, n, N_MIXERS, GROUP_W), g_group_out.reshape(N_MIXERS, GROUP_W))
    return y.reshape(b, n, D_MIX) @ w_out

def _hier_moe(h, w_rg, b_rg, w_re, b_re, w_up, w_down):
    group_p = jax.nn.softmax((h @ w_rg + b_rg).astype(jnp.float32), axis=-1)
    g_w, g_idx = lax.top_k(group_p, 1)
    e_logits = (h @ w_re + b_re).astype(jnp.float32).reshape(*h.shape[:-1], N_GROUPS, EXPERTS_PER_GROUP)
    e_logits = jnp.take_along_axis(e_logits, g_idx[..., None], axis=-2)[..., 0, :]
    e_w, e_idx = lax.top_k(jax.nn.softmax(e_logits, axis=-1), TOP_K)
    e_w = e_w / jnp.sum(e_w, axis=-1, keepdims=True)
    expert_id = g_idx * EXPERTS_PER_GROUP + e_idx
    combine = jnp.sum(jax.nn.one_hot(expert_id, N_EXPERTS, dtype=jnp.float32) * (g_w * e_w)[..., None],
                      axis=-2).astype(h.dtype)
    gate, up = jnp.split(jnp.einsum('bld,edf->blef', h, w_up), 2, axis=-1)
    return jnp.einsum('blef,efd->bld', jax.nn.silu(gate) * up * combine[..., None], w_down)

def _layer(x, xc, sc, scc, rope_c, rope_d, p, update_ctx):
    (w_mod, b_mod, g_attn_norm, w_in, sgu_v_gain, sgu_w, sgu_b, conv_w,
     gqa_q_gain, gqa_k_gain, mla_qa_gain, mla_w_qb, mla_kva_gain, mla_w_kvb,
     mla_q_gain, mla_k_gain, g_group_out, w_out, g_ffn_norm,
     w_rg, b_rg, w_re, b_re, w_up, w_down) = p
    shift1, scale1, gate1, shift2, scale2, gate2 = jnp.split((sc @ w_mod + b_mod)[:, None, :], 6, axis=-1)
    shift1c, scale1c, gate1c, shift2c, scale2c, gate2c = jnp.split(scc @ w_mod + b_mod, 6, axis=-1)

    h = _modulate(_rms_norm(x, g_attn_norm), shift1, scale1)
    hc = _modulate(_rms_norm(xc, g_attn_norm), shift1c, scale1c)
    a_u, a_v, b_b, b_c, b_x, c_q, c_k, c_v, d_cq, d_ckv, d_kr = jnp.split(h @ w_in, IN_SPLIT_IDX, axis=-1)
    (a_uc, a_vc, b_bc, b_cc, b_xc, c_qc, c_kc, c_vc,
     d_cqc, d_ckvc, d_krc) = jnp.split(hc @ w_in, IN_SPLIT_IDX, axis=-1)
    mla_p = (mla_qa_gain, mla_w_qb, mla_kva_gain, mla_w_kvb, mla_q_gain, mla_k_gain)

    qC_c, kC_c, vC_c = _gqa_qkv(c_qc, c_kc, c_vc, gqa_q_gain, gqa_k_gain, None)
    qD_c, kD_c, vD_c = _mla_qkv(d_cqc, d_ckvc, d_krc, *mla_p, None)
    qC, kC, vC = _gqa_qkv(c_q, c_k, c_v, gqa_q_gain, gqa_k_gain, rope_c)
    qD, kD, vD = _mla_qkv(d_cq, d_ckv, d_kr, *mla_p, rope_d)

    yC = _blocked_attention(qC, jnp.concatenate([kC_c, kC], axis=1), jnp.concatenate([vC_c, vC], axis=1), C_SCALE)
    yD = _blocked_attention(qD, jnp.concatenate([kD_c, kD], axis=1), jnp.concatenate([vD_c, vD], axis=1), D_SCALE)
    yA = _chunk_sgu(a_u, a_v, sgu_v_gain, sgu_w, sgu_b)
    yB = _short_conv(b_b, b_c, b_x, conv_w)
    x = x + gate1 * _merge_groups((yA, yB, yC, yD), g_group_out, w_out)
    x = x + gate2 * _hier_moe(_modulate(_rms_norm(x, g_ffn_norm), shift2, scale2),
                              w_rg, b_rg, w_re, b_re, w_up, w_down)

    if update_ctx:
        yc = _merge_groups((_chunk_sgu(a_uc, a_vc, sgu_v_gain, sgu_w, sgu_b),
                            _short_conv(b_bc, b_cc, b_xc, conv_w),
                            _attention(qC_c, kC_c, vC_c, C_SCALE),
                            _attention(qD_c, kD_c, vD_c, D_SCALE)), g_group_out, w_out)
        xc = xc + gate1c * yc
        xc = xc + gate2c * _hier_moe(_modulate(_rms_norm(xc, g_ffn_norm), shift2c, scale2c),
                                     w_rg, b_rg, w_re, b_re, w_up, w_down)
    return x, xc

def setup_inputs(seed: int = 0) -> dict:
    key = jax.random.key(seed)
    ks = jax.random.split(key, 32)
    L, D = DEPTH, D_MODEL
    f32 = jnp.float32

    def nrm(k, shape, scale):
        return jax.random.normal(k, shape, f32) * scale

    def gain(k, shape):
        return 1.0 + 0.05 * jax.random.normal(k, shape, f32)

    return {
        'x': nrm(ks[0], (BATCH, SEQ, D), 1.0),
        'c': nrm(ks[1], (BATCH, D), 1.0),
        'ctx': nrm(ks[2], (BATCH, CTX_LEN, D), 1.0),
        'c_ctx': nrm(ks[3], (D,), 1.0),
        'w_mod': nrm(ks[4], (L, D, 6 * D), 0.5 * D ** -0.5),
        'b_mod': nrm(ks[5], (L, 6 * D), 0.02),
        'g_attn_norm': gain(ks[6], (L, D)),
        'w_in': nrm(ks[7], (L, D, IN_COLS), D ** -0.5),
        'sgu_v_gain': gain(ks[8], (L, GROUP_W)),
        'sgu_w': nrm(ks[9], (L, A_HEADS, CHUNK, CHUNK), CHUNK ** -0.5),
        'sgu_b': gain(ks[10], (L, A_HEADS, CHUNK)),
        'conv_w': nrm(ks[11], (L, CONV_W, GROUP_W), CONV_W ** -0.5),
        'gqa_q_gain': gain(ks[12], (L, C_HEAD_DIM)),
        'gqa_k_gain': gain(ks[13], (L, C_HEAD_DIM)),
        'mla_qa_gain': gain(ks[14], (L, D_Q_LORA)),
        'mla_w_qb': nrm(ks[15], (L, D_Q_LORA, D_HEADS * (D_NOPE + D_ROPE)), D_Q_LORA ** -0.5),
        'mla_kva_gain': gain(ks[16], (L, D_KV_LORA)),
        'mla_w_kvb': nrm(ks[17], (L, D_KV_LORA, D_HEADS * (D_NOPE + D_V)), D_KV_LORA ** -0.5),
        'mla_q_gain': gain(ks[18], (L, D_NOPE + D_ROPE)),
        'mla_k_gain': gain(ks[19], (L, D_NOPE + D_ROPE)),
        'g_group_out': gain(ks[20], (L, D_MIX)),
        'w_out': nrm(ks[21], (L, D_MIX, D), D_MIX ** -0.5),
        'g_ffn_norm': gain(ks[22], (L, D)),
        'w_router_group': nrm(ks[23], (L, D, N_GROUPS), D ** -0.5),
        'b_router_group': nrm(ks[24], (L, N_GROUPS), 0.01),
        'w_router_expert': nrm(ks[25], (L, D, N_EXPERTS), D ** -0.5),
        'b_router_expert': nrm(ks[26], (L, N_EXPERTS), 0.01),
        'w_expert_up': nrm(ks[27], (L, N_EXPERTS, D, 2 * D_EXPERT), D ** -0.5),
        'w_expert_down': nrm(ks[28], (L, N_EXPERTS, D_EXPERT, D), D_EXPERT ** -0.5),
    }

def reference(x, c, ctx, c_ctx, w_mod, b_mod, g_attn_norm, w_in, sgu_v_gain, sgu_w, sgu_b, conv_w,
              gqa_q_gain, gqa_k_gain, mla_qa_gain, mla_w_qb, mla_kva_gain, mla_w_kvb, mla_q_gain,
              mla_k_gain, g_group_out, w_out, g_ffn_norm, w_router_group, b_router_group,
              w_router_expert, b_router_expert, w_expert_up, w_expert_down):
    rows = x.shape[1] // GRID_W
    rope_c = _axial_rope(rows, C_HEAD_DIM)
    rope_d = _axial_rope(rows, D_ROPE)
    sc = jax.nn.silu(c)
    scc = jax.nn.silu(c_ctx)
    xc = ctx
    for l in range(DEPTH):
        p = (w_mod[l], b_mod[l], g_attn_norm[l], w_in[l], sgu_v_gain[l], sgu_w[l], sgu_b[l], conv_w[l],
             gqa_q_gain[l], gqa_k_gain[l], mla_qa_gain[l], mla_w_qb[l], mla_kva_gain[l], mla_w_kvb[l],
             mla_q_gain[l], mla_k_gain[l], g_group_out[l], w_out[l], g_ffn_norm[l],
             w_router_group[l], b_router_group[l], w_router_expert[l], b_router_expert[l],
             w_expert_up[l], w_expert_down[l])
        x, xc = _layer(x, xc, sc, scc, rope_c, rope_d, p, l < DEPTH - 1)
    return x


_drawn_inputs = setup_inputs


def setup_inputs(seed=0):
    import zlib

    import numpy as np

    out = dict(_drawn_inputs(seed))
    spreads = {}
    factors = {'sgu_v_gain': 5.348,
     'sgu_b': 4.873,
     'gqa_q_gain': 8.0,
     'gqa_k_gain': 8.0,
     'mla_qa_gain': 8.0,
     'mla_kva_gain': 3.486,
     'mla_q_gain': 7.863,
     'mla_k_gain': 6.902,
     'b_router_group': 6.375,
     'b_router_expert': 8.0}
    for name, (base, spread) in spreads.items():
        noise = np.random.default_rng([zlib.crc32(name.encode()), seed]).standard_normal(out[name].shape)
        drawn = base * np.exp(spread * noise) if base else spread * noise
        out[name] = jnp.asarray(drawn.astype(out[name].dtype))
    for name, factor in factors.items():
        out[name] = (out[name] * factor).astype(out[name].dtype)
    return out
```

```python
import math
from contextlib import ExitStack

import concourse.bass as bass
from concourse import mybir

D = 1024
SEQ = 512
CTX = 256
DEPTH = 2
P = 128
KT = D // P
T = (SEQ + CTX) // P
TC = CTX // P
TOK = T * P
GW = 256
HEADS = 4
HD = 64
KVH = 2
ROPE = 32
DH = HD + ROPE
QLORA = 256
KVLORA = 128
NG = 4
NE = 16
EPG = NE // NG
FE = D // 4
EPS = 1e-6
GRID_W = 64
THETA = 10000.0
IN_COLS = 5 * GW + GW + 2 * 128 + QLORA + KVLORA + ROPE
C_AU, C_BB, C_BC, C_BX = 0, 2 * GW, 3 * GW, 4 * GW
C_CQ = 5 * GW
C_CK = C_CQ + GW
C_DQ = C_CK + 2 * KVH * HD
C_DKV = C_DQ + QLORA
KVC = 2 * KVH * HD + KVLORA + ROPE
UNIT = KT * 512
RING = 5
EXP_SLOTS = 3
EXP_F = KT * 512 + 2 * D
XT = TOK * 2 // P
NOV = XT - 1
ROWS = (NE + NOV + 1) * P
BIG = 1e30

V_BMOD, V_GA, V_GF, V_GO = 0, 48, 56, 64
V_QA, V_KVA, V_SB, V_CW = 72, 74, 75, 79
V_C, V_CC = 85, 93
V_ROWS = 101

K_ID, K_UP, K_ONE = 0, 128, 256
K_RC, K_RS = 384, 384 + 256
K_DC, K_DS = 896, 896 + 128
K_P4, K_P16, K_E, K_15E, K_V = 1152, 1156, 1172, 1188, 1204
K_IN4, K_IQ5, K_I8 = 1216, 1220, 1225
K_H = 1233
K_EPS = 1234
NCONST = 1236


def constants():
    import numpy as np
    c = np.zeros((P, NCONST), np.float32)
    c[:, K_ID:K_ID + P] = np.eye(P)
    c[:, K_UP:K_UP + P] = np.triu(np.ones((P, P)), 1)
    c[:, K_ONE:K_ONE + P] = 1.0
    pos = np.arange(SEQ)
    row, col = (pos // GRID_W).astype(np.float32), (pos % GRID_W).astype(np.float32)
    for width, kc, ks in ((HD, K_RC, K_RS), (ROPE, K_DC, K_DS)):
        nf = width // 4
        inv = np.float32(THETA) ** (-np.arange(nf, dtype=np.float32) / np.float32(nf))
        ang = np.concatenate([row[:, None] * inv, col[:, None] * inv], -1).astype(np.float32)
        cos = np.repeat(np.cos(ang), 2, -1)
        sin = np.repeat(np.sin(ang), 2, -1)
        sin[:, 0::2] *= -1
        c[:, kc:kc + 4 * width] = cos.reshape(4, P, width).transpose(1, 0, 2).reshape(P, -1)
        c[:, ks:ks + 4 * width] = sin.reshape(4, P, width).transpose(1, 0, 2).reshape(P, -1)
    c[:, K_P4:K_P4 + 4] = 4 - np.arange(4)
    c[:, K_P16:K_P16 + 16] = 16 - np.arange(16)
    c[:, K_E:K_E + 16] = np.arange(16)
    c[:, K_15E:K_15E + 16] = NE - 1 - np.arange(16)
    c[:, K_V:K_V + 12] = np.arange(12)
    c[:, K_IN4:K_IN4 + 4] = [1 / HD, 1 / HD, 1 / KVLORA, 1 / ROPE]
    c[:, K_IQ5:K_IQ5 + 5] = [1 / HD] * 4 + [1 / QLORA]
    c[:, K_I8:K_I8 + 8] = [1 / HD] * 4 + [1 / ROPE] * 4
    c[:, K_H] = -0.5
    return c


def block_kernel(nc, consts, x, c, ctx, c_ctx, w_mod, b_mod, g_attn_norm, w_in, sgu_v_gain, sgu_w,
                 sgu_b, conv_w, gqa_q_gain, gqa_k_gain, mla_qa_gain, mla_w_qb, mla_kva_gain,
                 mla_w_kvb, mla_q_gain, mla_k_gain, g_group_out, w_out, g_ffn_norm, w_rg, b_rg,
                 w_re, b_re, w_up, w_down, out):
    F32, I32 = mybir.dt.float32, mybir.dt.int32
    ALU, ACT, AX = mybir.AluOpType, mybir.ActivationFunctionType, mybir.AxisListType
    MUL, ADD, SUB = ALU.mult, ALU.add, ALU.subtract

    LAYERS = range(DEPTH)

    def full(l):
        return range(T) if l < DEPTH - 1 else range(TC, T)

    def an(l, t):
        return T * l + t

    def fn(l, t):
        return an(l, t) - TC * (l == DEPTH - 1)

    FULL = [(l, t) for l in LAYERS for t in full(l)]
    NF = {l: len(full(l)) for l in LAYERS}

    def keys(t):
        return CTX if t < TC else TOK

    NU = 2 * HEADS

    units = [("mod", 0, i) for i in range(4)] + [("kv", 0, 0), ("b", 0, 0), ("b", 0, 1), ("a", 0, 0)]
    units += [("mod", 0, i) for i in range(4, 12)] + [("q", 0, 0), ("o", 0, 0), ("o", 0, 1)]
    units += [("mod", 1, i) for i in range(12)]
    L0_UNITS = len(units)
    units += [("kv", 1, 0), ("b", 1, 0), ("b", 1, 1), ("a", 1, 0), ("q", 1, 0), ("o", 1, 0), ("o", 1, 1)]
    UI = {u: n for n, u in enumerate(units)}
    LAST_OF_LAYER = {0: L0_UNITS, 1: len(units)}

    es = ExitStack()
    with es:
        def sb(name, shape, dt=F32):
            return es.enter_context(nc.sbuf_tensor(name, shape, dt))

        def sem(name):
            return es.enter_context(nc.semaphore(name))

        wreg = sb("weights", [P, RING * UNIT])
        xb = sb("x_tile", [P, 2, D])
        hT = sb("h_transposed", [P, T, KT, P])
        kv = sb("keys_values", [P, 6144])
        yB = sb("y_conv", [P, 2, TOK])
        yA = sb("y_sgu", [P, T, GW])
        yn = sb("y_norm", [P, D])
        ynT = sb("y_norm_transposed", [P, KT, P])
        bc = sb("broadcast_rows", [P, 3, D])
        scr = sb("scratch", [P, 4, 784])
        yCD = sb("y_attention", [P, 2 * GW])
        cst = sb("constants", [P, NCONST])
        wqb = sb("mla_w_qb_s", [P, 2, HEADS * DH])
        wkvb = sb("mla_w_kvb_s", [P, 512])
        wsT = sb("sgu_w_transposed", [P, HEADS, P])
        wr = sb("w_router", [P, KT, NG + NE])
        rows = sb("row_vectors", [P, 600])
        vecT = sb("column_vectors", [P, DEPTH, V_ROWS])
        sT = sb("silu_c", [P, KT, 2])
        modc = sb("modulation", [P, DEPTH, 48, 2])
        a1 = sb("scale1", [P, DEPTH, KT, 2])
        a2 = sb("scale2", [P, DEPTH, KT, 2])
        qCT = sb("q_gqa_T", [P, 2, P])
        qDT = sb("q_mla_T", [P, HEADS, P])
        small = sb("small", [P, 400])
        posi = sb("positions", [P, T, 2], I32)
        ctl = sb("overflow_control", [P, 16], I32)

        kCT = kv[:, 0:768]
        kDT = kv[:, 768:768 + 3072].rearrange("p (h t) -> p h t", h=HEADS)
        vC = kv[:, 3840:3840 + 768].rearrange("p (t n) -> p t n", t=T)
        vD = kv[:, 4608:6144].rearrange("p (t n) -> p t n", t=T)
        G = [kv[:, s * D:(s + 1) * D] for s in range(3)]
        GT = [kv[:, (3 + s) * D:(4 + s) * D].rearrange("p (k n) -> p k n", k=KT) for s in range(3)]
        hTf = hT[:, :, :, :].rearrange("p t k n -> p t (k n)")
        yo = [hTf[:, s, :] for s in range(3)]
        yg = [[hTf[:, 2 * b + a, :] for a in range(2)] for b in range(2)]
        SC = [scr[:, i, :] for i in range(4)]
        scf = scr[:, :, :].rearrange("p a n -> p (a n)")
        zero = SC[3][:, 0:512]

        kSq, k2Sq = SC[0][:, 0:288], SC[0][:, 288:544]
        kCb = [SC[1][:, 0:128], SC[1][:, 128:256]]
        kRb = [SC[1][:, 256:288], SC[1][:, 288:320]]
        kTmp = SC[1][:, 320:576]
        kDb = SC[2][:, 0:HEADS * DH].rearrange("p (h n) -> p h n", h=HEADS)
        kLora, kLoraT = SC[2][:, 384:512], SC[2][:, 512:640]
        cvC, cvZ, cvA = SC[0], SC[1], SC[2]
        gb = [SC[0][:, 0:512], SC[1][:, 0:512]]
        gSq, gMix = SC[2][:, 0:256], SC[2][:, 256:512]
        qC = SC[0][:, 0:256]
        qD = SC[0][:, 256:640].rearrange("p (h n) -> p h n", h=HEADS)
        loraT = SC[1][:, 0:256].rearrange("p (k n) -> p k n", k=2)
        qSq = SC[2][:, 0:512]
        qTmp, lora = SC[3][:, 0:256], SC[3][:, 256:512]
        PB = [SC[0], SC[1]]
        PT = [SC[2], SC[3]]
        sg = [scf[:, s * 256:(s + 1) * 256] for s in range(3)]
        av = [scf[:, (3 + s) * 256:(4 + s) * 256] for s in range(3)]
        aT = [scf[:, (6 + s) * 256:(7 + s) * 256].rearrange("p (k n) -> p k n", k=2) for s in range(3)]
        junk = bc[:, 0, :]
        junkf = scf[:, 0:D]

        rpos = [0]

        def rbuf(n):
            rpos[0] += n
            return scf[:, rpos[0] - n:rpos[0]]

        def r3(n):
            return rbuf(T * n).rearrange("p (t n) -> p t n", t=T)

        r_max, r_oh, r_sc, r_dif, r_sum, r_w1 = r3(1), r3(4), r3(4), r3(4), r3(1), r3(1)
        r_L, r_neg, r_t16, r_oh1, r_oh2, r_m1, r_m2 = r3(16), r3(4), r3(16), r3(16), r3(16), r3(1), r3(1)
        r_M, r_pre, r_rank_, r_j, r_row = r3(16), r3(16), r3(16), r3(16), r3(16)
        r_tot, r_cnt, r_nov, r_end, r_ovb, r_one = [rbuf(16) for _ in range(6)]
        r_cmp = rbuf(12 * 16).rearrange("p (v e) -> p v e", v=12)
        r_ctl = rbuf(16)
        r_pf = r3(2)

        nss, nrs = small[:, 0:2], small[:, 2:4]
        kss, krs = [small[:, 4:8], small[:, 8:12]], [small[:, 12:16], small[:, 16:20]]
        k2ss, k2rs = [small[:, 20:24], small[:, 24:28]], [small[:, 28:32], small[:, 32:36]]
        ass, ars = [small[:, 36:40], small[:, 40:44]], [small[:, 44:48], small[:, 48:52]]
        qss, qrs, q2ss, q2rs = small[:, 52:57], small[:, 57:62], small[:, 62:70], small[:, 70:78]
        mss, mrs, fss, frs = small[:, 78:82], small[:, 82:86], small[:, 86:87], small[:, 87:88]
        nmax, esum, rinv = small[:, 88:96], small[:, 96:104], small[:, 104:112]
        logits = small[:, 256:376].rearrange("p (t n) -> p t n", t=T)
        wts = small[:, 376:388].rearrange("p (t a) -> p t a", t=T)

        def ring(n):
            return wreg[:, (n % RING) * UNIT:(n % RING + 1) * UNIT]

        def rview(n, cols):
            return ring(n)[:, 0:KT * cols].rearrange("p (k n) -> p k n", k=KT)

        def eup(s):
            return wreg[:, s * EXP_F:s * EXP_F + KT * 512].rearrange("p (k n) -> p k n", k=KT)

        def edn(s):
            return wreg[:, s * EXP_F + KT * 512:(s + 1) * EXP_F].rearrange("p (k n) -> p k n", k=2)

        ident = cst[:, K_ID:K_ID + P]
        R_SGU, R_CQ, R_CK, R_MQ, R_MK, R_RB = 0, 256, 320, 384, 480, 576

        ps = [es.enter_context(nc.psum_tensor(f"ps{i}", [P, 1024], F32)) for i in range(4)]

        def bank(i):
            return ps[i // 2][:, (i % 2) * 512:(i % 2) * 512 + 512]

        xmid = nc.dram_tensor("x_mid", [DEPTH, TOK, D], F32, kind="Internal").ap()
        xnext = nc.dram_tensor("x_next", [TOK, D], F32, kind="Internal").ap()
        hs = nc.dram_tensor("h_sorted", [ROWS, D], F32, kind="Internal").ap()
        ys = nc.dram_tensor("y_sorted", [ROWS, D], F32, kind="Internal").ap()

        hsv, ysv = [v.rearrange("(e p) d -> e p d", p=P) for v in (hs, ys)]
        N_ZERO = ROWS // P // 4 + (ROWS // P - NE) // 4

        const_in = sem("const_in")
        vec_in = sem("vec_in")
        rowv_in = sem("rowv_in")
        smallw_in = sem("smallw_in")
        vec_tp = sem("vec_tp")
        vec_ok = sem("vec_ok")
        ws_tp = sem("ws_tp")
        ws_ok = sem("ws_ok")
        kvx_in, qx_in, bx_in = sem("kv_unit_tail"), sem("q_unit_tail"), [sem("conv_unit_tail0"), sem("conv_unit_tail1")]
        unit_in = [sem(f"unit_in{i}") for i in range(RING)]
        mod_u = sem("mod_u")
        mod_ok = sem("mod_ok")
        x_in = [sem("x_in0"), sem("x_in1")]
        n_sq, n_rs, n_xn, n_tp, n_evd, n_eva = [sem(f"norm_{s}") for s in ("sq", "rs", "xn", "tp", "evd", "eva")]
        k_ps, k_sq, k_ss, k_rs, k_nrm, k_lT, k_lTs = [sem(f"kv_{s}") for s in ("ps", "sq", "ss", "rs", "nrm", "loraT", "loraTs")]
        k2_ps, k2_sq, k2_ss, k2_rs, k2_nrm, k_all, k_tp, k_tpd, k_tpa = [
            sem(f"kv2_{s}") for s in ("ps", "sq", "ss", "rs", "nrm", "all", "tp", "tpd", "tpa")]
        b_ps, b_c, b_ok = [sem(f"conv_{s}") for s in ("ps", "c", "ok")]
        a_ps, a_gelu, a_ss, a_rs, a_v, a_mix, a_ok = [sem(f"sgu_{s}") for s in ("ps", "gelu", "ss", "rs", "v", "mix", "ok")]
        bc_ps, bc_ok = sem("bc_ps"), sem("bc_ok")
        q_ps, q_sq, q_ss, q_rs, q_lora, q_lT, q_lTs = [sem(f"q_{s}") for s in ("ps", "sq", "ss", "rs", "lora", "loraT", "loraTs")]
        q2_ps, q2_sq, q2_ss, q2_rs, q2_nrm, q_all, q_tp, q_tpd, q_tpa = [
            sem(f"q2_{s}") for s in ("ps", "sq", "ss", "rs", "nrm", "all", "tp", "tpd", "tpa")]
        s_ps, s_mx, s_p, p_tp, p_evd, p_eva, o_ps, o_ok = [
            sem(f"att_{s}") for s in ("scores", "max", "probs", "tp", "evd", "eva", "pv", "out")]
        yb_tp, m_sq, m_rs, m_yn, m_tp, m_evd, m_eva, op_ps, x1_ok = [
            sem(f"merge_{s}") for s in ("conv_tp", "sq", "rs", "yn", "tp", "evd", "eva", "out", "x1")]
        f_sq, f_rs, f_h2, f_tp, f_evd, f_eva, lg_ps, lg_ok = [
            sem(f"ffn_{s}") for s in ("sq", "rs", "h2", "tp", "evd", "eva", "logits", "logits_ok")]
        x1_st = sem("x1_stored")
        zero_ok, zero_st = sem("zero_ok"), sem("zero_stored")
        r_exp_in, r_exp, r_m, r_rank, r_pos = [sem(f"route_{s}") for s in ("exp_in", "exp", "mask", "rank", "pos")]
        sc_done = sem("rows_scattered")
        ew_in = [sem(f"expert_w{s}") for s in range(3)]
        g_in = [sem(f"expert_rows{s}") for s in range(3)]
        g_tp, g_evd, g_eva, e_up, e_sg, e_a, e_aT, e_aTs, e_dn, e_yd, e_ya = [
            sem(f"expert_{s}") for s in ("tp", "evd", "eva", "up", "sg", "a", "aT", "aTs", "dn", "yd", "ya")]
        y_st = [sem(f"expert_stored{s}") for s in range(3)]
        STEP = dict(tp=1, ev=3, up=4, sg=5, a=6, aT=7, aTs=8, dn=9, y=11)
        STEPS = 11
        ov = {}
        for l in LAYERS:
            ov[l] = {s: sem(f"ov{l}_{s}") for s in ("w", "g", "step", "st", "end")}
        c_in = [sem("comb_in0"), sem("comb_in1")]
        c_ok, c_st = sem("comb_ok"), sem("comb_stored")
        dve_ch, pool_ch = sem("dve_chain"), sem("pool_chain")

        xuse = {}
        for l in LAYERS:
            for t in range(T):
                xuse["n", l, t] = len(xuse)
            for t in full(l):
                xuse["u", l, t] = len(xuse)
            for t in full(l):
                xuse["c", l, t] = len(xuse)

        in_slot = [(NE - s + 2) // 3 for s in range(3)]

        def x_tile(kind, l, t):
            return xb[:, xuse[kind, l, t] % 2, :]

        def x_arrived(eng, kind, l, t):
            q = xuse[kind, l, t]
            eng.wait_ge(x_in[q % 2], 16 * (q // 2 + 1))

        def unit_arrived(eng, u):
            n = UI[u]
            eng.wait_ge(unit_in[n % RING], 16 * (n // RING + 1))

        def unit_released(eng, n):
            kind, l, i = units[n]
            if kind == "mod":
                eng.wait_ge(mod_u, 12 * l + i + 1)
            elif kind == "kv":
                eng.wait_ge(k_ps, T * (l + 1))
            elif kind == "b":
                eng.wait_ge(b_ps, 2 * l + i + 1)
            elif kind == "a":
                eng.wait_ge(a_ps, fn(l, T - 1) + 1)
            elif kind == "q":
                eng.wait_ge(q_ps, fn(l, T - 1) + 1)
            else:
                eng.wait_ge(op_ps, fn(l, T - 1) + 1)

        def seg(t0, t1):
            return slice(t0 * P, t1 * P)

        ZC, ZL = 1, CTX + 2
        block = es.enter_context(nc.Block())

        @block.sync
        def _(sp):
            def load_unit(n):
                kind, l, i = units[n]
                if n >= L0_UNITS and units[n - RING][1] == 0:
                    sp.wait_ge(e_dn, NE)
                    sp.wait_ge(ov[0]["end"], 1)
                elif n >= RING:
                    unit_released(sp, n - RING)
                done = unit_in[n % RING]
                wi = w_in[l].rearrange("(k p) n -> p k n", p=P)
                if kind == "mod":
                    sp.dma_start(rview(n, 512), w_mod[l].rearrange("(k p) n -> p k n", p=P)[:, :, i * 512:(i + 1) * 512]).then_inc(done, 16)
                elif kind == "a":
                    sp.dma_start(rview(n, 512), wi[:, :, C_AU:C_AU + 512]).then_inc(done, 16)
                elif kind == "o":
                    sp.dma_start(rview(n, 512), w_out[l].rearrange("(k p) n -> p k n", p=P)[:, :, i * 512:(i + 1) * 512]).then_inc(done, 16)
                elif kind == "kv":
                    v = rview(n, KVC)
                    sp.dma_start(v[:, :, 0:256], wi[:, :, C_CK:C_CK + 256]).then_inc(done, 16)
                    sp.dma_start(v[:, :, 256:KVC], wi[:, :, C_DKV:C_DKV + KVLORA + ROPE]).then_inc(kvx_in, 16)
                elif kind == "q":
                    v = rview(n, 512)
                    sp.dma_start(v[:, :, 0:256], wi[:, :, C_CQ:C_CQ + 256]).then_inc(done, 16)
                    sp.dma_start(v[:, :, 256:512], wi[:, :, C_DQ:C_DQ + 256]).then_inc(qx_in, 16)
                else:
                    v = rview(n, 384)
                    for c3 in range(3):
                        c0 = C_BB + c3 * GW + i * P
                        sp.dma_start(v[:, :, c3 * P:(c3 + 1) * P], wi[:, :, c0:c0 + P]).then_inc(done if c3 == 0 else bx_in[i], 16)

            def load_x(kind, l, t):
                q = xuse[kind, l, t]
                if kind in "nu":
                    src = (ctx[0, t * P:(t + 1) * P, :] if t < TC else x[0, (t - TC) * P:(t - TC + 1) * P, :]) \
                        if l == 0 else xnext[t * P:(t + 1) * P, :]
                else:
                    src = xmid[l, t * P:(t + 1) * P, :]
                sp.dma_start(xb[:, q % 2, :], src).then_inc(x_in[q % 2], 16)

            def store_x(l, t):
                dst = xnext[t * P:(t + 1) * P, :] if l + 1 < DEPTH else out[0, (t - TC) * P:(t - TC + 1) * P, :]
                sp.dma_start(dst, x_tile("c", l, t)).then_inc(c_st, 16)

            sp.dma_start(cst[:, :], consts).then_inc(const_in, 16)
            for l in LAYERS:
                st = scr[0:P, l, 0:P]
                for r, src, n in ((V_BMOD, b_mod, 48), (V_GA, g_attn_norm, 8), (V_GF, g_ffn_norm, 8),
                                  (V_GO, g_group_out, 8), (V_QA, mla_qa_gain, 2), (V_KVA, mla_kva_gain, 1)):
                    sp.dma_start(st[r:r + n, :], src[l].rearrange("(r n) -> r n", n=P)).then_inc(vec_in, 16)
                sp.dma_start(st[V_SB:V_SB + 4, :], sgu_b[l]).then_inc(vec_in, 16)
                sp.dma_start(st[V_CW:V_CW + 6, :], conv_w[l].rearrange("w (j n) -> (w j) n", n=P)).then_inc(vec_in, 16)
                sp.dma_start(st[V_C:V_C + 8, :], c[0].rearrange("(r n) -> r n", n=P)).then_inc(vec_in, 16)
                sp.dma_start(st[V_CC:V_CC + 8, :], c_ctx.rearrange("(r n) -> r n", n=P)).then_inc(vec_in, 16)

            def load_small(l):
                for o, src, n in ((R_SGU, sgu_v_gain, 256), (R_CQ, gqa_q_gain, 64), (R_CK, gqa_k_gain, 64),
                                  (R_MQ, mla_q_gain, 96), (R_MK, mla_k_gain, 96), (R_RB, b_rg, 4), (R_RB + 4, b_re, 16)):
                    sp.dma_start(rows[:, o:o + n], src[l].rearrange("(a n) -> a n", a=1).to_broadcast([P, n])).then_inc(rowv_in, 16)
                sp.dma_start(wqb[:, :, :], mla_w_qb[l].rearrange("(k p) n -> p k n", p=P)).then_inc(smallw_in, 16)
                sp.dma_start(wkvb[:, :], mla_w_kvb[l]).then_inc(smallw_in, 16)
                sp.dma_start(wr[:, :, 0:NG], w_rg[l].rearrange("(k p) n -> p k n", p=P)).then_inc(smallw_in, 16)
                sp.dma_start(wr[:, :, NG:], w_re[l].rearrange("(k p) n -> p k n", p=P)).then_inc(smallw_in, 16)
                sp.dma_start(ynT[:, 0:HEADS, :], sgu_w[l].rearrange("h i j -> i h j")).then_inc(smallw_in, 16)

            def norm_loads(l, first):
                for t in range(first, T):
                    n = an(l, t)
                    if t >= 2:
                        sp.wait_ge(n_xn, n - 1)
                    load_x("n", l, t)

            load_unit(0)
            load_x("n", 0, 0)
            load_x("n", 0, 1)
            load_small(0)
            for n in range(1, RING):
                load_unit(n)
            norm_loads(0, 2)
            for n in range(RING, UI["mod", 1, 2]):
                load_unit(n)
                if units[n] == ("b", 0, 1):
                    sp.wait_ge(zero_ok, 1)
                    zh, zy = [v.rearrange("(a p b) d -> a p b d", p=P, b=4) for v in (hs, ys)]
                    for dst in [zh[a] for a in range(ROWS // P // 4)] + [zy[a] for a in range(NE // 4, ROWS // P // 4)]:
                        sp.dma_start(dst.rearrange("p b (c n) -> p (b c) n", n=512),
                                     zero.rearrange("p (a n) -> p a n", a=1).to_broadcast([P, 8, 512])).then_inc(zero_st, 16)

            for l in LAYERS:
                if l:
                    sp.wait_ge(c_st, 16 * NF[0])
                    load_x("n", l, 0)
                    load_x("n", l, 1)
                    for n in range(L0_UNITS, L0_UNITS + RING):
                        load_unit(n)
                    norm_loads(l, 2)
                    for n in range(L0_UNITS + RING, len(units)):
                        load_unit(n)
                for t in full(l):
                    f = fn(l, t)
                    if t == full(l)[0]:
                        sp.wait_ge(n_xn, an(l, T - 1) + 1)
                    if t >= full(l)[0] + 2:
                        sp.wait_ge(x1_st, 16 * (f - 1))
                        sp.wait_ge(f_h2, f - 1)
                    load_x("u", l, t)
                    if t > full(l)[0]:
                        sp.wait_ge(x1_ok, f)
                        sp.dma_start(xmid[l, (t - 1) * P:t * P, :], x_tile("u", l, t - 1)).then_inc(x1_st, 16)
                sp.wait_ge(x1_ok, fn(l, T - 1) + 1)
                sp.dma_start(xmid[l, (T - 1) * P:T * P, :], x_tile("u", l, T - 1)).then_inc(x1_st, 16)
                if l == 0:
                    for n in range(UI["mod", 1, 2], L0_UNITS):
                        load_unit(n)

                last = LAST_OF_LAYER[l]

                def load_expert(e, s):
                    sp.dma_start(eup(s), w_up[l, e].rearrange("(k p) n -> p k n", p=P)).then_inc(ew_in[s], 16)
                    sp.dma_start(edn(s), w_down[l, e].rearrange("(k p) n -> p k n", p=P)).then_inc(ew_in[s], 16)

                for s, slots in enumerate(((0, 1), (1, 2), (3, 4))):
                    for r in slots:
                        unit_released(sp, max(n for n in range(last) if n % RING == r))
                    load_expert(s, s)
                sp.wait_ge(sc_done, 16 * 2 * (fn(l, T - 1) + 1))
                for s in range(3):
                    sp.dma_start(G[s], hsv[s]).then_inc(g_in[s], 16)

                def store_y(i, s):
                    sp.wait_ge(e_yd, i * 3 + (NE * l + s + 2))
                    sp.wait_ge(e_ya, i * 3 + (NE * l + s + 2))
                    sp.dma_start(ysv[i * 3 + s], yo[s]).then_inc(y_st[s], 16)

                with sp.Fori(0, (NE - 1) // 3 - 1) as i:
                    for s in range(3):
                        sp.wait_ge(e_dn, i * 3 + (NE * l + s + 1))
                        e = i * 3 + (s + 3)
                        sp.dma_start(G[s], hsv[e]).then_inc(g_in[s], 16)
                        sp.dma_start(eup(s), w_up[l, e].rearrange("(k p) n -> p k n", p=P)).then_inc(ew_in[s], 16)
                        sp.dma_start(edn(s), w_down[l, e].rearrange("(k p) n -> p k n", p=P)).then_inc(ew_in[s], 16)
                        store_y(i, s)
                sp.wait_ge(e_dn, NE * l + NE - 3)
                sp.dma_start(G[0], hsv[NE - 1]).then_inc(g_in[0], 16)
                load_expert(NE - 1, 0)
                for s in range(3):
                    store_y((NE - 1) // 3 - 1, s)
                if l == 0:
                    sp.wait_ge(lg_ok, fn(0, T - 1) + 1)
                    load_small(1)
                store_y((NE - 1) // 3, 0)

                sp.wait_ge(r_pos, l + 1)
                v = nc.sync.value_load(ctl[0:1, 12:13], min_val=0, max_val=NOV)
                o = ov[l]
                for s in range(3):
                    sp.wait_ge(y_st[s], 16 * in_slot[s] * (l + 1))
                sp.sem_inc(o["st"], 16)
                with sp.If(v > 0):
                    with sp.Fori(0, v) as i:
                        e = nc.sync.value_load(ctl[0:1, bass.ds(i, 1)], min_val=0, max_val=NE - 1)
                        sp.wait_ge(o["st"], i * 16 + 16)
                        sp.dma_start(G[0], hsv[i + NE]).then_inc(o["g"], 16)
                        sp.dma_start(eup(0), w_up[l, e].rearrange("(k p) n -> p k n", p=P)).then_inc(o["w"], 16)
                        sp.dma_start(edn(0), w_down[l, e].rearrange("(k p) n -> p k n", p=P)).then_inc(o["w"], 16)
                        sp.wait_ge(o["step"], i * STEPS + STEP["y"])
                        sp.dma_start(ysv[i + NE], yo[0]).then_inc(o["st"], 16)
                sp.wait_ge(o["st"], v * 16 + 16)
                sp.sem_inc(o["end"], 1)

                for t in full(l):
                    f = fn(l, t)
                    if t == full(l)[0]:
                        sp.wait_ge(x1_st, 16 * (fn(l, T - 1) + 1))
                        sp.wait_ge(f_h2, fn(l, T - 1) + 1)
                    if t >= full(l)[0] + 2:
                        sp.wait_ge(c_st, 16 * (f - 1))
                    load_x("c", l, t)
                    if t > full(l)[0]:
                        sp.wait_ge(c_ok, f)
                        store_x(l, t - 1)
                sp.wait_ge(c_ok, fn(l, T - 1) + 1)
                store_x(l, T - 1)
            sp.wait_ge(c_st, 16 * len(FULL))
            sp.wait_ge(zero_st, 16 * N_ZERO)

        @block.gpsimd
        def _(pool):
            chain = [0]

            def link(ins):
                chain[0] += 1
                ins.then_inc(pool_ch, 1)
                pool.wait_ge(pool_ch, chain[0])

            pool.sem_inc(e_yd, 1)
            pool.sem_inc(e_ya, 1)
            pool.memset(zero, 0.0).then_inc(zero_ok, 1)
            half = cst[:, K_H:K_H + 1]

            def rsqrt(out, ss, n, inv):
                if isinstance(inv, float):
                    link(pool.tensor_scalar(ss, ss, inv, EPS, MUL, ADD))
                else:
                    link(pool.tensor_tensor(ss, ss, inv, MUL))
                    link(pool.tensor_scalar(ss, ss, EPS, None, ADD))
                return pool.tensor_tensor(out, ss, half.to_broadcast([P, n]), ALU.pow)

            def rope(x4, heads, width, kc, ks, t, tmp):
                cos = cst[:, kc + (t - TC) * width:kc + (t - TC + 1) * width].rearrange("p (a n) -> p a n", a=1).to_broadcast([P, heads, width])
                sin = cst[:, ks + (t - TC) * width:ks + (t - TC + 1) * width]
                tm = tmp[:, 0:heads * width].rearrange("p (h n b) -> p h n b", h=heads, b=2)
                xs = x4.rearrange("p h (n b) -> p h n b", b=2)
                sv = sin.rearrange("p (n b) -> p n b", b=2)
                for b in range(2):
                    link(pool.tensor_tensor(tm[:, :, :, b], xs[:, :, :, 1 - b],
                                            sv[:, :, b].rearrange("p (a n) -> p a n", a=1).to_broadcast([P, heads, width // 2]), MUL))
                link(pool.tensor_tensor(x4, x4, cos, MUL))
                return pool.tensor_tensor(x4, x4, tmp[:, 0:heads * width].rearrange("p (h n) -> p h n", h=heads), ADD)

            pool.wait_ge(const_in, 16)

            for l in LAYERS:
                lastf = fn(l, T - 1)
                for i in range(T + 3):
                    if i < T:
                        n = an(l, i)
                        pool.wait_ge(n_sq, n + 1)
                        rsqrt(nrs[:, n % 2:n % 2 + 1], nss[:, n % 2:n % 2 + 1], 1, 1.0 / D).then_inc(n_rs, 1)
                    if 0 <= i - 1 < T:
                        n = an(l, i - 1)
                        pool.wait_ge(k_ss, n + 1)
                        rsqrt(krs[n % 2], kss[n % 2], 4, cst[:, K_IN4:K_IN4 + 4]).then_inc(k_rs, 1)
                    if 0 <= i - 2 < T:
                        n = an(l, i - 2)
                        pool.wait_ge(k2_ss, n + 1)
                        rsqrt(k2rs[n % 2], k2ss[n % 2], 4, 1.0 / HD).then_inc(k2_rs, 1)
                    if 0 <= i - 3 < T:
                        t = i - 3
                        n = an(l, t)
                        pool.wait_ge(k2_nrm, n + 1)
                        if t >= TC:
                            link(rope(kCb[n % 2].rearrange("p (h n) -> p h n", h=KVH), KVH, HD, K_RC, K_RS, t, kTmp))
                            link(rope(kRb[n % 2].rearrange("p (h n) -> p h n", h=1), 1, ROPE, K_DC, K_DS, t, kTmp))
                        pool.tensor_copy(kDb[:, :, HD:DH], kRb[n % 2].rearrange("p (a n) -> p a n", a=1).to_broadcast([P, HEADS, ROPE])).then_inc(k_all, 1)
                for t in full(l):
                    f = fn(l, t)
                    pool.wait_ge(a_ss, f + 1)
                    rsqrt(ars[f % 2], ass[f % 2], 4, 1.0 / HD).then_inc(a_rs, 1)
                for t in full(l):
                    f = fn(l, t)
                    if f == 0:
                        pool.wait_ge(zero_st, 16 * N_ZERO)
                    pool.wait_ge(q_ss, f + 1)
                    rsqrt(qrs, qss, 5, cst[:, K_IQ5:K_IQ5 + 5]).then_inc(q_rs, 1)
                    pool.wait_ge(q2_ss, f + 1)
                    rsqrt(q2rs, q2ss, 8, cst[:, K_I8:K_I8 + 8]).then_inc(q2_rs, 1)
                    pool.wait_ge(q2_nrm, f + 1)
                    if t >= TC:
                        link(rope(qC.rearrange("p (h n) -> p h n", h=HEADS), HEADS, HD, K_RC, K_RS, t, qTmp))
                        rope(qD[:, :, HD:DH], HEADS, ROPE, K_DC, K_DS, t, qTmp).then_inc(q_all, 1)
                    else:
                        pool.sem_inc(q_all, 1)
                    pool.wait_ge(m_sq, f + 1)
                    rsqrt(mrs, mss, 4, 1.0 / GW).then_inc(m_rs, 1)
                    pool.wait_ge(f_sq, f + 1)
                    rsqrt(frs, fss, 1, 1.0 / D).then_inc(f_rs, 1)

                pool.wait_ge(r_pos, l + 1)
                for t in full(l):
                    for a in range(2):
                        pool.indirect_dma_start(out=hs, out_offset=bass.IndirectOffsetOnAxis(ap=posi[:, t, a:a + 1], axis=0),
                                                in_=hTf[:, t, :], in_offset=None).then_inc(sc_done, 16)
                pool.wait_ge(sc_done, 16 * 2 * (lastf + 1))

                for s in range(3):
                    pool.wait_ge(y_st[s], 16 * in_slot[s] * (l + 1))
                pool.wait_ge(ov[l]["end"], 1)

                for t in full(l):
                    f = fn(l, t)
                    if t >= full(l)[0] + 2:
                        pool.wait_ge(c_ok, f - 1)
                    for a in range(2):
                        pool.indirect_dma_start(out=yg[f % 2][a], out_offset=None, in_=ys,
                                                in_offset=bass.IndirectOffsetOnAxis(ap=posi[:, t, a:a + 1], axis=0)).then_inc(c_in[f % 2], 16)

        @block.scalar
        def _(act):
            def copy(out, in_):
                return act.activation(out, in_, ACT.Copy)

            act.wait_ge(vec_tp, 1)
            for l in LAYERS:
                copy(vecT[:, l, :], bank(6 + l)[:, 0:V_ROWS])
            act.activation(sT[:, :, 0], bank(6)[:, V_CC:V_CC + KT], ACT.Silu)
            act.activation(sT[:, :, 1], bank(6)[:, V_C:V_C + KT], ACT.Silu).then_inc(vec_ok, 1)

            for l in LAYERS:
                act.wait_ge(ws_tp, l + 1)
                copy(wsT[:, :, :], bank(0).rearrange("p (h n) -> p h n", h=HEADS)).then_inc(ws_ok, 1)
                for i in range(T + 3):
                    if i < T:
                        n = an(l, i)
                        x_arrived(act, "n", l, i)
                        if n >= 2:
                            act.wait_ge(n_rs, n - 1)
                        act.activation(junk, x_tile("n", l, i), ACT.Square,
                                       accum_out=nss[:, n % 2:n % 2 + 1]).then_inc(n_sq, 1)
                    if 0 <= i - 1 < T:
                        n = an(l, i - 1)
                        kps = bank(4 + n % 2)
                        act.wait_ge(k_ps, n + 1)
                        copy(vC[:, i - 1, :], kps[:, 128:256])
                        act.wait_ge(k_ss, n)
                        act.activation(kSq[:, 0:128], kps[:, 0:128], ACT.Square)
                        act.activation(kSq[:, 128:288], kps[:, 256:416], ACT.Square).then_inc(k_sq, 1)
                    if 0 <= i - 2 < T:
                        n = an(l, i - 2)
                        act.wait_ge(k_lT, n + 1)
                        act.wait_ge(k2_ps, n)
                        act.activation(kLoraT, bank(6)[:, 0:P], ACT.Copy,
                                       scale=vecT[:, l, V_KVA:V_KVA + 1]).then_inc(k_lTs, 1)
                        k2 = bank(7).rearrange("p (h n) -> p h n", h=HEADS)
                        act.wait_ge(k2_ps, n + 1)
                        copy(vD[:, i - 2, :].rearrange("p (h n) -> p h n", h=HEADS), k2[:, :, HD:2 * HD])
                        act.wait_ge(k2_ss, n)
                        act.activation(k2Sq.rearrange("p (h n) -> p h n", h=HEADS), k2[:, :, 0:HD], ACT.Square).then_inc(k2_sq, 1)
                    if 0 <= i - 3 < T:
                        n = an(l, i - 3)
                        act.wait_ge(k_tp, n + 1)
                        copy(kCT[:, (i - 3) * P:(i - 2) * P], bank(2)[:, 0:P]).then_inc(k_tpa, 1)
                    if i < T:
                        n = an(l, i)
                        s = int(i >= TC)
                        act.wait_ge(n_tp, n + 1)
                        act.wait_ge(mod_ok, 2 * l + 1)
                        for k in range(4, KT):
                            last = act.activation(hT[:, i, k, :], ps[0][:, k * P:(k + 1) * P], ACT.Identity,
                                                  bias=modc[:, l, k, s:s + 1], scale=a1[:, l, k, s:s + 1])
                        last.then_inc(n_eva, 1)
                for j in range(2):
                    b = 2 * l + j
                    act.wait_ge(b_ps, b + 1)
                    act.wait_ge(b_ok, b)
                    if l == 0:
                        copy(cvC[:, 0:CTX], bank(3)[:, 0:CTX])
                    copy(cvC[:, CTX:TOK], bank(2)).then_inc(b_c, 1)
                for t in full(l):
                    f = fn(l, t)
                    act.wait_ge(a_ps, f + 1)
                    if f >= 2:
                        act.wait_ge(a_ok, f - 1)
                    act.activation(gb[f % 2], bank(6 + f % 2), ACT.Gelu_apprx_tanh).then_inc(a_gelu, 1)

                def broadcast_evac(b0, n, s0):
                    for v in range(n):
                        act.wait_ge(bc_ps, b0 + v + 1)
                        copy(bc[:, s0 + v, :], ps[1 + v % 2][:, :]).then_inc(bc_ok, 1)

                bcn = 8 * l
                for t in full(l):
                    f = fn(l, t)
                    if t in (0, TC):
                        broadcast_evac(bcn, 3, 0)
                        bcn += 3
                    act.wait_ge(q_ps, f + 1)
                    act.activation(qSq, bank(6), ACT.Square).then_inc(q_sq, 1)
                    act.wait_ge(q_lT, f + 1)
                    for k in range(2):
                        last = act.activation(loraT[:, k, :], bank(7)[:, k * P:(k + 1) * P], ACT.Copy,
                                              scale=vecT[:, l, V_QA + k:V_QA + k + 1])
                    last.then_inc(q_lTs, 1)
                    act.wait_ge(q2_ps, f + 1)
                    act.activation(qSq[:, 0:HEADS * DH], bank(4)[:, 0:HEADS * DH], ACT.Square).then_inc(q2_sq, 1)
                    act.wait_ge(q_tp, f + 1)
                    copy(qCT[:, :, :], bank(0)[:, 0:256].rearrange("p (g n) -> p g n", g=2)).then_inc(q_tpa, 1)

                    nk = keys(t)

                    def exp(u):
                        w = NU * f + u
                        act.wait_ge(s_mx, w + 1)
                        if w >= 2:
                            act.wait_ge(p_tp, w - 1)
                        act.activation(PB[u % 2][:, 0:nk], ps[u % 2][:, 0:nk], ACT.Exp, bias=nmax[:, u:u + 1],
                                       accum_out=esum[:, u:u + 1]).then_inc(s_p, 1)

                    exp(0)
                    for u in range(NU):
                        w = NU * f + u
                        if u + 1 < NU:
                            exp(u + 1)
                        act.wait_ge(p_tp, w + 1)
                        if w >= 2:
                            act.wait_ge(o_ps, w - 1)
                        copy(PT[u % 2][:, nk // 2:nk], bank(5)[:, 0:nk // 2]).then_inc(p_eva, 1)

                    act.wait_ge(yb_tp, f + 1)
                    act.wait_ge(o_ok, NU * (f + 1))
                    for g, src in enumerate((yA[:, t, :], ps[2][:, 0:GW], yCD[:, 0:GW], yCD[:, GW:])):
                        last = act.activation(junkf[:, g * GW:(g + 1) * GW], src, ACT.Square, accum_out=mss[:, g:g + 1])
                    last.then_inc(m_sq, 1)
                    act.wait_ge(m_tp, f + 1)
                    for k in range(4, KT):
                        last = act.activation(ynT[:, k, :], ps[0][:, k * P:(k + 1) * P], ACT.Copy,
                                              scale=vecT[:, l, V_GO + k:V_GO + k + 1])
                    last.then_inc(m_eva, 1)
                    act.wait_ge(x1_ok, f + 1)
                    act.wait_ge(m_sq, f + 1)
                    act.activation(junkf, x_tile("u", l, t), ACT.Square, accum_out=fss).then_inc(f_sq, 1)
                    act.wait_ge(f_tp, f + 1)
                    copy(ynT[:, 4:, :], ps[2][:, 512:].rearrange("p (k n) -> p k n", k=4)).then_inc(f_eva, 1)

                t0 = full(l)[0]
                act.wait_ge(r_exp_in, 2 * l + 1)
                act.activation(r_dif[:, t0:, :], r_dif[:, t0:, :], ACT.Exp).then_inc(r_exp, 1)
                act.wait_ge(r_exp_in, 2 * l + 2)
                act.activation(r_m2[:, t0:, :], r_m2[:, t0:, :], ACT.Exp).then_inc(r_exp, 1)
                if l == 0:
                    broadcast_evac(bcn, 2, 0)
                else:
                    broadcast_evac(bcn, 1, 1)

                def rows_evac(count, s):
                    act.wait_ge(g_tp, count)
                    copy(GT[s][:, 4:, :], ps[0][:, 512:].rearrange("p (k n) -> p k n", k=4)).then_inc(g_eva, 1)

                def expert(i, s, more, first=False):
                    e1 = i * 3 + (NE * l + s + 1)
                    act.wait_ge(e_up, e1)
                    act.activation(sg[s], bank(2)[:, 0:FE], ACT.Silu).then_inc(e_sg, 1)
                    if more:
                        rows_evac(e1 + 1, (s + 1) % 3)
                    act.wait_ge(e_aT, e1)
                    copy(aT[s], bank(3)[:, 0:FE].rearrange("p (k n) -> p k n", k=2)).then_inc(e_aTs, 1)
                    act.wait_ge(e_dn, e1)
                    if l or not first:
                        act.wait_ge(y_st[s], i * 16 + 16 * in_slot[s] * l)
                    copy(yo[s][:, 512:], bank(5)).then_inc(e_ya, 1)

                rows_evac(NE * l + 1, 0)
                for s in range(3):
                    expert(0, s, True, first=True)
                with act.Fori(1, (NE - 1) // 3) as i:
                    for s in range(3):
                        expert(i, s, True)
                expert((NE - 1) // 3, 0, False)

                o = ov[l]
                v = nc.scalar.value_load(ctl[0:1, 12:13], min_val=0, max_val=NOV)
                with act.If(v > 0):
                    with act.Fori(0, v) as i:
                        act.wait_ge(o["step"], i * STEPS + STEP["tp"])
                        copy(GT[0][:, 4:, :], ps[0][:, 512:].rearrange("p (k n) -> p k n", k=4)).then_inc(o["step"], 1)
                        act.wait_ge(o["step"], i * STEPS + STEP["up"])
                        act.activation(sg[0], bank(2)[:, 0:FE], ACT.Silu).then_inc(o["step"], 1)
                        act.wait_ge(o["step"], i * STEPS + STEP["aT"])
                        copy(aT[0], bank(3)[:, 0:FE].rearrange("p (k n) -> p k n", k=2)).then_inc(o["step"], 1)
                        act.wait_ge(o["step"], i * STEPS + STEP["dn"])
                        copy(yo[0][:, 512:], bank(5)).then_inc(o["step"], 1)

        @block.vector
        def _(dve):
            chain = [0]

            def link(ins):
                chain[0] += 1
                ins.then_inc(dve_ch, 1)
                dve.wait_ge(dve_ch, chain[0])

            def tt(out, a, b, op):
                return dve.tensor_tensor(out, a, b, op)

            def ts(out, a, s1, s2, op0, op1=None):
                return dve.tensor_scalar(out, a, s1, s2, op0) if op1 is None else dve.tensor_scalar(out, a, s1, s2, op0, op1)

            def each(v, n):
                return v.rearrange("p (h a) -> p h a", a=1).to_broadcast([P, v.shape[1], n])

            def over(v, h):
                return v.rearrange("p (a n) -> p a n", a=1).to_broadcast([P, h, v.shape[1]])

            def heads(v, h):
                return v.rearrange("p (h n) -> p h n", h=h)

            def total(out, in_):
                return dve.tensor_reduce(out, in_, AX.X, ADD)

            def modulation(l, half):
                c0, c1 = (0, 16) if half == 0 else (16, 48)
                dve.wait_ge(mod_u, 4 if (l, half) == (0, 0) else 12 * (l + 1))
                m = bank(7)[:, 2 * c0:2 * c1].rearrange("p (c s) -> p c s", s=2)
                link(tt(modc[:, l, c0:c1, :], m, each(vecT[:, l, V_BMOD + c0:V_BMOD + c1], 2), ADD))
                dst, sc, g = (a1, 8, V_GA) if half == 0 else (a2, 32, V_GF)
                link(ts(dst[:, l, :, :], modc[:, l, sc:sc + KT, :], 1.0, None, ADD))
                tt(dst[:, l, :, :], dst[:, l, :, :], each(vecT[:, l, g:g + KT], 2), MUL).then_inc(mod_ok, 1)

            dve.wait_ge(vec_ok, 1)
            modulation(0, 0)
            for l in LAYERS:
                dve.wait_ge(rowv_in, 16 * 7 * (l + 1))
                ts(rows[:, R_CQ:R_CQ + HD], rows[:, R_CQ:R_CQ + HD], HD ** -0.5, None, MUL)
                link(ts(rows[:, R_MQ:R_MQ + DH], rows[:, R_MQ:R_MQ + DH], DH ** -0.5, None, MUL))
                dve.wait_ge(mod_ok, 2 * l + 1)
                for i in range(T + 3):
                    if i < T:
                        n = an(l, i)
                        s = int(i >= TC)
                        dve.wait_ge(n_rs, n + 1)
                        dve.wait_ge(n_tp, n)
                        ts(yn[:, :], x_tile("n", l, i), nrs[:, n % 2:n % 2 + 1], None, MUL).then_inc(n_xn, 1)
                        dve.wait_ge(n_tp, n + 1)
                        for k in range(4):
                            last = ts(hT[:, i, k, :], ps[0][:, k * P:(k + 1) * P],
                                      a1[:, l, k, s:s + 1], modc[:, l, k, s:s + 1], MUL, ADD)
                        last.then_inc(n_evd, 1)
                    if 0 <= i - 1 < T:
                        n = an(l, i - 1)
                        dve.wait_ge(k_sq, n + 1)
                        total(kss[n % 2][:, 0:2], heads(kSq[:, 0:128], 2))
                        total(kss[n % 2][:, 2:3], kSq[:, 128:256])
                        total(kss[n % 2][:, 3:4], kSq[:, 256:288]).then_inc(k_ss, 1)
                    if 0 <= i - 3 < T:
                        n = an(l, i - 3)
                        dve.wait_ge(k2_rs, n + 1)
                        dve.wait_ge(k_tp, n)
                        link(tt(kDb[:, :, 0:HD], heads(bank(7), HEADS)[:, :, 0:HD], each(k2rs[n % 2], HD), MUL))
                        tt(kDb[:, :, 0:HD], kDb[:, :, 0:HD], over(rows[:, R_MK:R_MK + HD], HEADS), MUL).then_inc(k2_nrm, 1)
                    if 0 <= i - 2 < T:
                        n = an(l, i - 2)
                        kps, r, kc = bank(4 + n % 2), krs[n % 2], heads(kCb[n % 2], 2)
                        dve.wait_ge(k_rs, n + 1)
                        dve.wait_ge(k_lT, n)
                        if n >= 2:
                            dve.wait_ge(k_tp, n - 1)
                        ts(kLora, kps[:, 256:384], r[:, 2:3], None, MUL)
                        link(tt(kc, heads(kps[:, 0:128], 2), each(r[:, 0:2], HD), MUL))
                        tt(kc, kc, over(rows[:, R_CK:R_CK + HD], 2), MUL)
                        dve.scalar_tensor_tensor(kRb[n % 2], kps[:, 384:416], r[:, 3:4],
                                                 rows[:, R_MK + HD:R_MK + DH], MUL, MUL).then_inc(k_nrm, 1)
                        dve.wait_ge(k2_sq, n + 1)
                        total(k2ss[n % 2], heads(k2Sq, HEADS)).then_inc(k2_ss, 1)
                    if 0 <= i - 3 < T:
                        n = an(l, i - 3)
                        dve.wait_ge(k_tp, n + 1)
                        dve.tensor_copy(kDT[0:DH, :, (i - 3) * P:(i - 2) * P], heads(bank(3), HEADS)[0:DH]).then_inc(k_tpd, 1)

                lo, zl = (0, ZC) if l == 0 else (CTX, ZL)
                if l == 0:
                    width = TOK + 1
                else:
                    width = SEQ
                for j in range(2):
                    b = 2 * l + j
                    wc = [vecT[:, l, V_CW + 2 * w + j:V_CW + 2 * w + j + 1] for w in range(3)]
                    dve.wait_ge(b_c, b + 1)
                    for z in (0, ZL - 1, ZL + SEQ):
                        dve.memset(cvZ[:, z:z + 1], 0.0)
                    if l == 0:
                        tt(cvZ[:, ZC:ZC + CTX], cvC[:, 0:CTX], bank(5)[:, 0:CTX], MUL)
                    link(tt(cvZ[:, ZL:ZL + SEQ], cvC[:, CTX:TOK], bank(4), MUL))
                    link(ts(cvA[:, 0:width], cvZ[:, zl - 1:zl - 1 + width], wc[0], None, MUL))
                    link(dve.scalar_tensor_tensor(cvA[:, 0:width], cvZ[:, zl:zl + width], wc[1], cvA[:, 0:width], MUL, ADD))
                    link(dve.scalar_tensor_tensor(cvA[:, 0:width], cvZ[:, zl + 1:zl + 1 + width], wc[2], cvA[:, 0:width], MUL, ADD))
                    if l == 0:
                        tt(yB[:, j, 0:CTX], cvA[:, 0:CTX], bank(1)[:, 0:CTX], MUL)
                    tt(yB[:, j, CTX:TOK], cvA[:, ZL - zl:ZL - zl + SEQ], bank(0), MUL).then_inc(b_ok, 1)

                tl = list(full(l))
                for i in range(len(tl) + 1):
                    if i < len(tl):
                        f = fn(l, tl[i])
                        dve.wait_ge(a_gelu, f + 1)
                        dve.wait_ge(a_ss, f)
                        link(tt(gSq, gb[f % 2][:, GW:], gb[f % 2][:, GW:], MUL))
                        total(ass[f % 2], heads(gSq, HEADS)).then_inc(a_ss, 1)
                    if i:
                        t = tl[i - 1]
                        f = fn(l, t)
                        v = heads(gb[f % 2][:, GW:], HEADS)
                        dve.wait_ge(a_rs, f + 1)
                        link(tt(v, v, each(ars[f % 2], HD), MUL))
                        tt(v, v, heads(rows[:, R_SGU:R_SGU + GW], HEADS), MUL).then_inc(a_v, 1)
                        dve.wait_ge(a_mix, f + 1)
                        link(tt(heads(gMix, HEADS), heads(bank(4 + f % 2)[:, 0:GW], HEADS), each(vecT[:, l, V_SB:V_SB + 4], HD), ADD))
                        tt(yA[:, t, :], gMix, gb[f % 2][:, 0:GW], MUL).then_inc(a_ok, 1)

                if l == 0:
                    modulation(0, 1)
                for t in full(l):
                    f = fn(l, t)
                    q = bank(6)
                    dve.wait_ge(q_sq, f + 1)
                    total(qss[:, 0:4], heads(qSq[:, 0:256], HEADS))
                    total(qss[:, 4:5], qSq[:, 256:512]).then_inc(q_ss, 1)
                    dve.wait_ge(q_rs, f + 1)
                    ts(lora, q[:, 256:512], qrs[:, 4:5], None, MUL).then_inc(q_lora, 1)
                    link(tt(qC.rearrange("p (g v n) -> p v g n", g=2, v=2), q[:, 0:256].rearrange("p (v g n) -> p v g n", g=2, v=2),
                            qrs[:, 0:4].rearrange("p (v g a) -> p v g a", v=2, a=1).to_broadcast([P, 2, 2, HD]), MUL))
                    link(tt(heads(qC, HEADS), heads(qC, HEADS), over(rows[:, R_CQ:R_CQ + HD], HEADS), MUL))
                    dve.wait_ge(q2_sq, f + 1)
                    sq = heads(qSq[:, 0:HEADS * DH], HEADS)
                    total(q2ss[:, 0:4], sq[:, :, 0:HD])
                    total(q2ss[:, 4:8], sq[:, :, HD:DH]).then_inc(q2_ss, 1)
                    dve.wait_ge(q2_rs, f + 1)
                    q2 = heads(bank(4)[:, 0:HEADS * DH], HEADS)
                    tt(qD[:, :, 0:HD], q2[:, :, 0:HD], each(q2rs[:, 0:4], HD), MUL)
                    link(tt(qD[:, :, HD:DH], q2[:, :, HD:DH], each(q2rs[:, 4:8], ROPE), MUL))
                    tt(qD, qD, over(rows[:, R_MQ:R_MQ + DH], HEADS), MUL).then_inc(q2_nrm, 1)
                    dve.wait_ge(q_tp, f + 1)
                    dve.tensor_copy(qDT[0:DH, :, :], heads(bank(1), HEADS)[0:DH]).then_inc(q_tpd, 1)

                    nk = keys(t)

                    def row_max(u):
                        w = NU * f + u
                        dve.wait_ge(s_ps, w + 1)
                        dve.tensor_reduce(nmax[:, u:u + 1], ps[u % 2][:, 0:nk], AX.X, ALU.max, negate=True).then_inc(s_mx, 1)

                    def head_out(u):
                        w = NU * f + u
                        dve.wait_ge(o_ps, w + 1)
                        link(dve.reciprocal(rinv[:, u:u + 1], esum[:, u:u + 1]))
                        ts(yCD[:, u * HD:(u + 1) * HD], bank(6 + u % 2)[:, 0:HD], rinv[:, u:u + 1], None, MUL).then_inc(o_ok, 1)

                    row_max(0)
                    for u in range(NU):
                        w = NU * f + u
                        if u + 1 < NU:
                            row_max(u + 1)
                        dve.wait_ge(p_tp, w + 1)
                        if w >= 2:
                            dve.wait_ge(o_ps, w - 1)
                        dve.tensor_copy(PT[u % 2][:, 0:nk // 2], bank(4)[:, 0:nk // 2]).then_inc(p_evd, 1)
                        if u:
                            head_out(u - 1)
                    head_out(NU - 1)

                    dve.wait_ge(m_rs, f + 1)
                    for g, src in enumerate((yA[:, t, :], ps[2][:, 0:GW], yCD[:, 0:GW], yCD[:, GW:])):
                        last = ts(yn[:, g * GW:(g + 1) * GW], src, mrs[:, g:g + 1], None, MUL)
                    last.then_inc(m_yn, 1)
                    dve.wait_ge(m_tp, f + 1)
                    for k in range(4):
                        last = ts(ynT[:, k, :], ps[0][:, k * P:(k + 1) * P], vecT[:, l, V_GO + k:V_GO + k + 1], None, MUL)
                    last.then_inc(m_evd, 1)
                    dve.wait_ge(op_ps, f + 1)
                    dve.wait_ge(bc_ok, 3 if t < TC else 6 if l == 0 else 11)
                    xt = x_tile("u", l, t)
                    x_arrived(dve, "u", l, t)
                    link(tt(yn[:, :], ps[1][:, :], bc[:, 2, :], MUL))
                    tt(xt, xt, yn[:, :], ADD).then_inc(x1_ok, 1)
                    dve.wait_ge(f_rs, f + 1)
                    h2 = hTf[:, t, :]
                    link(dve.scalar_tensor_tensor(h2, xt, frs, bc[:, 0, :], MUL, MUL))
                    tt(h2, h2, bc[:, 1, :], ADD).then_inc(f_h2, 1)
                    dve.wait_ge(f_tp, f + 1)
                    dve.tensor_copy(ynT[:, 0:4, :], ps[2][:, 0:512].rearrange("p (k n) -> p k n", k=4)).then_inc(f_evd, 1)
                    dve.wait_ge(lg_ps, f + 1)
                    tt(logits[:, t, :], bank(7)[:, 0:NG + NE], rows[:, R_RB:R_RB + NG + NE], ADD).then_inc(lg_ok, 1)

                t0 = full(l)[0]
                nt = NF[l]
                U = slice(t0, T)

                def rv(v):
                    return v[:, U, :]

                def along(v, n):
                    return rv(v).to_broadcast([P, nt, n])

                def row(c0, n):
                    return cst[:, c0:c0 + n].rearrange("p (a n) -> p a n", a=1).to_broadcast([P, nt, n])

                def first_max(oh, vals, best, scr_, pref, n):
                    link(dve.tensor_reduce(rv(best), vals, AX.X, ALU.max))
                    link(tt(rv(scr_), vals, along(best, n), ALU.is_ge))
                    link(tt(rv(scr_), rv(scr_), row(pref, n), MUL))
                    link(dve.tensor_reduce(rv(r_sum), rv(scr_), AX.X, ALU.max))
                    link(tt(rv(oh), rv(scr_), along(r_sum, n), ALU.is_equal))

                lg = logits[:, U, :]
                dve.wait_ge(lg_ok, fn(l, T - 1) + 1)
                first_max(r_oh, lg[:, :, 0:NG], r_max, r_sc, K_P4, NG)
                tt(rv(r_dif), lg[:, :, 0:NG], along(r_max, NG), SUB).then_inc(r_exp_in, 1)
                link(ts(rv(r_neg), rv(r_oh), BIG, -BIG, MUL, ADD))
                for t in full(l):
                    last = tt(heads(r_L[:, t, :], NG), heads(logits[:, t, NG:], NG), each(r_neg[:, t, :], EPG), ADD)
                link(last)
                first_max(r_oh1, rv(r_L), r_m1, r_t16, K_P16, NE)
                link(ts(rv(r_t16), rv(r_oh1), -4 * BIG, None, MUL))
                link(tt(rv(r_L), rv(r_L), rv(r_t16), ADD))
                first_max(r_oh2, rv(r_L), r_m2, r_t16, K_P16, NE)
                tt(rv(r_m2), rv(r_m2), rv(r_m1), SUB).then_inc(r_exp_in, 1)
                dve.memset(r_pre[:, t0, :], 0.0)
                link(tt(rv(r_M), rv(r_oh1), rv(r_oh2), ADD))
                for t in range(t0 + 1, T):
                    link(tt(r_pre[:, t, :], r_pre[:, t - 1, :], r_M[:, t - 1, :], ADD))
                tt(r_tot, r_pre[:, T - 1, :], r_M[:, T - 1, :], ADD).then_inc(r_m, 1)
                dve.wait_ge(r_exp, 2 * l + 2)
                link(dve.tensor_reduce(rv(r_sum), rv(r_dif), AX.X, ADD))
                link(ts(rv(r_w1), rv(r_m2), 1.0, None, ADD))
                link(tt(rv(r_w1), rv(r_w1), rv(r_sum), MUL))
                link(dve.reciprocal(wts[:, U, 0:1], rv(r_w1)))
                link(tt(wts[:, U, 1:2], wts[:, U, 0:1], rv(r_m2), MUL))
                dve.wait_ge(r_rank, l + 1)
                dve.tensor_copy(rv(r_rank_), bank(6)[:, 0:nt * NE].rearrange("p (t e) -> p t e", e=NE))
                link(dve.tensor_copy(r_cnt, bank(6)[:, T * NE:T * NE + NE]))
                link(ts(r_nov, r_cnt, float(P), None, ALU.is_gt))
                link(ts(rv(r_j), rv(r_rank_), float(P), None, ALU.is_ge))
                for m in range(2, T):
                    link(dve.scalar_tensor_tensor(rv(r_j), rv(r_rank_), float(m * P), rv(r_j), ALU.is_ge, ADD))
                    link(dve.scalar_tensor_tensor(r_nov, r_cnt, float(m * P), r_nov, ALU.is_gt, ADD))
                link(dve.memset(r_one, 1.0))
                link(dve.tensor_tensor_scan(r_end, r_one, r_nov, 0.0, MUL, ADD))
                link(tt(r_ovb, r_end, r_nov, SUB))
                link(tt(r_ovb, r_ovb, cst[:, K_15E:K_15E + NE], ADD))
                link(tt(rv(r_t16), rv(r_j), over(r_ovb, nt), ADD))
                link(ts(rv(r_row), rv(r_j), 0.0, None, ALU.is_gt))
                link(tt(rv(r_t16), rv(r_t16), rv(r_row), MUL))
                link(tt(rv(r_t16), rv(r_t16), row(K_E, NE), ADD))
                link(tt(rv(r_t16), rv(r_t16), rv(r_j), SUB))
                link(dve.scalar_tensor_tensor(rv(r_row), rv(r_t16), float(P), rv(r_rank_), MUL, ADD))
                for a, oh in enumerate((r_oh1, r_oh2)):
                    link(tt(rv(r_t16), rv(oh), rv(r_row), MUL))
                    link(total(r_pf[:, U, a:a + 1], rv(r_t16)))
                dve.tensor_copy(posi[:, U, :], rv(r_pf))
                link(tt(r_cmp, over(r_end, 12), each(cst[:, K_V:K_V + 12], NE), ALU.is_le))
                link(total(r_ctl[:, 0:12], r_cmp))
                link(ts(r_ctl[:, 0:12], r_ctl[:, 0:12], float(NE - 1), None, ALU.min))
                link(dve.tensor_copy(r_ctl[:, 12:13], r_end[:, NE - 1:NE]))
                dve.tensor_copy(ctl[:, 0:13], r_ctl[:, 0:13]).then_inc(r_pos, 1)

                if l + 1 < DEPTH:
                    modulation(l + 1, 0)
                    modulation(l + 1, 1)

                def rows_evac(count, s):
                    dve.wait_ge(g_tp, count)
                    dve.tensor_copy(GT[s][:, 0:4, :], ps[0][:, 0:512].rearrange("p (k n) -> p k n", k=4)).then_inc(g_evd, 1)

                def expert(i, s, more, first=False):
                    e1 = i * 3 + (NE * l + s + 1)
                    dve.wait_ge(e_sg, e1)
                    tt(av[s], sg[s], bank(2)[:, FE:2 * FE], MUL).then_inc(e_a, 1)
                    if more:
                        rows_evac(e1 + 1, (s + 1) % 3)
                    dve.wait_ge(e_dn, e1)
                    if l or not first:
                        dve.wait_ge(y_st[s], i * 16 + 16 * in_slot[s] * l)
                    dve.tensor_copy(yo[s][:, 0:512], bank(4)).then_inc(e_yd, 1)

                rows_evac(NE * l + 1, 0)
                for s in range(3):
                    expert(0, s, True, first=True)
                with dve.Fori(1, (NE - 1) // 3) as i:
                    for s in range(3):
                        expert(i, s, True)
                expert((NE - 1) // 3, 0, False)

                o = ov[l]
                v = nc.vector.value_load(ctl[0:1, 12:13], min_val=0, max_val=NOV)
                with dve.If(v > 0):
                    with dve.Fori(0, v) as i:
                        dve.wait_ge(o["step"], i * STEPS + STEP["tp"])
                        dve.tensor_copy(GT[0][:, 0:4, :], ps[0][:, 0:512].rearrange("p (k n) -> p k n", k=4)).then_inc(o["step"], 1)
                        dve.wait_ge(o["step"], i * STEPS + STEP["sg"])
                        tt(av[0], sg[0], bank(2)[:, FE:2 * FE], MUL).then_inc(o["step"], 1)
                        dve.wait_ge(o["step"], i * STEPS + STEP["dn"])
                        dve.tensor_copy(yo[0][:, 0:512], bank(4)).then_inc(o["step"], 1)

                for t in full(l):
                    f = fn(l, t)
                    y1, y2 = yg[f % 2]
                    dve.wait_ge(c_in[f % 2], 32 * (f // 2 + 1))
                    if t == t0:
                        dve.wait_ge(bc_ok, 8 if l == 0 else 12)
                    link(ts(y1, y1, wts[:, t, 0:1], None, MUL))
                    link(dve.scalar_tensor_tensor(y1, y2, wts[:, t, 1:2], y1, MUL, ADD))
                    link(tt(y1, y1, bc[:, int(t >= TC), :], MUL))
                    x_arrived(dve, "c", l, t)
                    xt = x_tile("c", l, t)
                    tt(xt, xt, y1, ADD).then_inc(c_ok, 1)

        @block.tensor
        def _(pe):
            def mm(out, lhsT, rhs, start=True, stop=True):
                return pe.matmul(out, lhsT, rhs, start=start, stop=stop)

            def tp(out, in_, n=P):
                return pe.transpose(out, in_, ident[0:n, 0:n])

            def modulation(l, i0, i1):
                for i in range(i0, i1):
                    n = UI["mod", l, i]
                    unit_arrived(pe, ("mod", l, i))
                    w = rview(n, 512)
                    for c4 in range(4):
                        cc = 4 * i + c4
                        for k in range(KT):
                            last = mm(bank(7)[:, 2 * cc:2 * cc + 2], w[:, k, c4 * P:(c4 + 1) * P], sT[:, k, :], k == 0, k == KT - 1)
                    last.then_inc(mod_u, 1)

            def broadcast(l, b0, vecs, s_of):
                for v, (src, c0) in enumerate(vecs):
                    pe.wait_ge(bc_ok, b0 + v - 1) if b0 + v >= 2 else None
                    s = s_of[v]
                    for k in range(KT):
                        last = mm(ps[1 + v % 2][:, k * P:(k + 1) * P], src[:, l, c0 + k, s:s + 1].to_broadcast([P, P]), ident)
                    last.then_inc(bc_ps, 1)

            pe.wait_ge(const_in, 16)
            pe.wait_ge(vec_in, 16 * 10 * DEPTH)
            for l in LAYERS:
                last = tp(bank(6 + l)[:, 0:V_ROWS], scr[0:V_ROWS, l, 0:P], V_ROWS)
            last.then_inc(vec_tp, 1)
            pe.wait_ge(vec_ok, 1)
            modulation(0, 0, 4)

            for l in LAYERS:
                pe.wait_ge(smallw_in, 16 * 5 * (l + 1))
                for h in range(HEADS):
                    last = tp(bank(0)[:, h * P:(h + 1) * P], ynT[:, h, :])
                last.then_inc(ws_tp, 1)
                pe.wait_ge(ws_ok, l + 1)
                ukv = UI["kv", l, 0]
                for i in range(T + 3):
                    if i < T:
                        n = an(l, i)
                        pe.wait_ge(n_xn, n + 1)
                        pe.wait_ge(n_evd, n)
                        pe.wait_ge(n_eva, n)
                        for k in range(KT):
                            last = tp(ps[0][:, k * P:(k + 1) * P], yn[:, k * P:(k + 1) * P])
                        last.then_inc(n_tp, 1)
                    if 0 <= i - 1 < T:
                        n = an(l, i - 1)
                        pe.wait_ge(n_evd, n + 1)
                        pe.wait_ge(n_eva, n + 1)
                        if i == 1:
                            unit_arrived(pe, ("kv", l, 0))
                            pe.wait_ge(kvx_in, 16 * (l + 1))
                        if n >= 2:
                            pe.wait_ge(k_nrm, n - 1)
                        for k in range(KT):
                            last = mm(bank(4 + n % 2)[:, 0:KVC], hT[:, i - 1, k, :], rview(ukv, KVC)[:, k, :], k == 0, k == KT - 1)
                        last.then_inc(k_ps, 1)
                    if 0 <= i - 2 < T:
                        n = an(l, i - 2)
                        pe.wait_ge(k_nrm, n + 1)
                        pe.wait_ge(k_lTs, n)
                        tp(bank(6)[:, 0:P], kLora).then_inc(k_lT, 1)
                        pe.wait_ge(k_lTs, n + 1)
                        pe.wait_ge(k2_nrm, n)
                        if n == 0:
                            pe.wait_ge(mod_ok, 1)
                        mm(bank(7), kLoraT, wkvb[:, :]).then_inc(k2_ps, 1)
                    if 0 <= i - 3 < T:
                        n = an(l, i - 3)
                        pe.wait_ge(k_all, n + 1)
                        pe.wait_ge(k_tpa, n)
                        pe.wait_ge(k_tpd, n)
                        tp(bank(2)[:, 0:P], kCb[n % 2])
                        for h in range(HEADS):
                            last = tp(bank(3)[0:DH, h * P:(h + 1) * P], kDb[:, h, :])
                        last.then_inc(k_tp, 1)

                pe.wait_ge(k_tpa, T * (l + 1))
                pe.wait_ge(k_tpd, T * (l + 1))
                for j in range(2):
                    unit_arrived(pe, ("b", l, j))
                    pe.wait_ge(bx_in[j], 32 * (l + 1))
                    pe.wait_ge(b_ok, 2 * l + j)
                    w = rview(UI["b", l, j], 384)
                    for c3 in range(3):
                        for k in range(KT):
                            last = mm(bank(2 * c3).rearrange("p (t n) -> p t n", n=P), w[:, k, c3 * P:(c3 + 1) * P], hT[:, TC:T, k, :], k == 0, k == KT - 1)
                        if l == 0:
                            for k in range(KT):
                                last = mm(bank(2 * c3 + 1)[:, 0:CTX].rearrange("p (t n) -> p t n", n=P), w[:, k, c3 * P:(c3 + 1) * P], hT[:, 0:TC, k, :], k == 0, k == KT - 1)
                    last.then_inc(b_ps, 1)

                pe.wait_ge(b_ok, 2 * (l + 1))
                unit_arrived(pe, ("a", l, 0))
                w = rview(UI["a", l, 0], 512)
                tl = list(full(l))
                for i in range(len(tl) + 1):
                    if i < len(tl):
                        f = fn(l, tl[i])
                        if f >= 2:
                            pe.wait_ge(a_gelu, f - 1)
                        for k in range(KT):
                            last = mm(bank(6 + f % 2), hT[:, tl[i], k, :], w[:, k, :], k == 0, k == KT - 1)
                        last.then_inc(a_ps, 1)
                    if i:
                        f = fn(l, tl[i - 1])
                        pe.wait_ge(a_v, f + 1)
                        if f >= 2:
                            pe.wait_ge(a_ok, f - 1)
                        for h in range(HEADS):
                            last = mm(bank(4 + f % 2)[:, h * HD:(h + 1) * HD], wsT[:, h, :], gb[f % 2][:, GW + h * HD:GW + (h + 1) * HD])
                        last.then_inc(a_mix, 1)

                pe.wait_ge(a_ok, fn(l, T - 1) + 1)
                if l == 0:
                    pe.wait_ge(a_gelu, fn(l, T - 1) + 1)
                    modulation(0, 4, 12)
                pe.wait_ge(mod_ok, 2 * (l + 1))
                bcn = 8 * l
                for t in full(l):
                    f = fn(l, t)
                    if t in (0, TC):
                        if f:
                            pe.wait_ge(lg_ok, f)
                        s = int(t >= TC)
                        broadcast(l, bcn, ((a2, 0), (modc, 24), (modc, 16)), (s, s, s))
                        bcn += 3
                        pe.wait_ge(bc_ok, bcn)
                    if f:
                        pe.wait_ge(lg_ok, f)
                    if t == tl[0]:
                        unit_arrived(pe, ("q", l, 0))
                        pe.wait_ge(qx_in, 16 * (l + 1))
                    w = rview(UI["q", l, 0], 512)
                    for k in range(KT):
                        last = mm(bank(6), hT[:, t, k, :], w[:, k, :], k == 0, k == KT - 1)
                    last.then_inc(q_ps, 1)
                    pe.wait_ge(q_lora, f + 1)
                    for k in range(2):
                        last = tp(bank(7)[:, k * P:(k + 1) * P], lora[:, k * P:(k + 1) * P])
                    last.then_inc(q_lT, 1)
                    pe.wait_ge(q_lTs, f + 1)
                    for k in range(2):
                        last = mm(bank(4)[:, 0:HEADS * DH], loraT[:, k, :], wqb[:, k, :], k == 0, k == 1)
                    last.then_inc(q2_ps, 1)
                    pe.wait_ge(q_all, f + 1)
                    for g in range(2):
                        tp(bank(0)[:, g * P:(g + 1) * P], qC[:, g * P:(g + 1) * P])
                    for h in range(HEADS):
                        last = tp(bank(1)[0:DH, h * P:(h + 1) * P], qD[:, h, :])
                    last.then_inc(q_tp, 1)
                    pe.wait_ge(q_tpa, f + 1)
                    pe.wait_ge(q_tpd, f + 1)

                    nk = keys(t)

                    def scores(u):
                        w = NU * f + u
                        if u >= 2:
                            pe.wait_ge(s_p, w - 1)
                        if u < HEADS:
                            v, g = u // 2, u % 2
                            q, kk = qCT[v * HD:(v + 1) * HD, g, :], kCT[v * HD:(v + 1) * HD, :]
                        else:
                            q, kk = qDT[0:DH, u - HEADS, :], kDT[0:DH, u - HEADS, :]
                        for c0 in range(0, nk, 512):
                            c1 = min(c0 + 512, nk)
                            last = mm(ps[u % 2][:, c0:c1], q, kk[:, c0:c1])
                        last.then_inc(s_ps, 1)

                    scores(0)
                    for u in range(NU):
                        w = NU * f + u
                        if u + 1 < NU:
                            scores(u + 1)
                        pe.wait_ge(s_p, w + 1)
                        pe.wait_ge(p_evd, w)
                        pe.wait_ge(p_eva, w)
                        for k in range(nk // P):
                            hf, kk = divmod(k, nk // P // 2)
                            last = tp(bank(4 + hf)[:, kk * P:(kk + 1) * P], PB[u % 2][:, k * P:(k + 1) * P])
                        last.then_inc(p_tp, 1)
                        pe.wait_ge(p_evd, w + 1)
                        pe.wait_ge(p_eva, w + 1)
                        if w >= 2:
                            pe.wait_ge(o_ok, w - 1)
                        for k in range(nk // P):
                            vv = vC[:, k, (u // 2) * HD:(u // 2 + 1) * HD] if u < HEADS else vD[:, k, (u - HEADS) * HD:(u - HEADS + 1) * HD]
                            last = mm(bank(6 + u % 2)[:, 0:HD], PT[u % 2][:, k * P:(k + 1) * P], vv, k == 0, k == nk // P - 1)
                        last.then_inc(o_ps, 1)

                    for j in range(2):
                        last = tp(ps[2][:, j * P:(j + 1) * P], yB[:, j, t * P:(t + 1) * P])
                    last.then_inc(yb_tp, 1)
                    pe.wait_ge(m_yn, f + 1)
                    for k in range(KT):
                        last = tp(ps[0][:, k * P:(k + 1) * P], yn[:, k * P:(k + 1) * P])
                    last.then_inc(m_tp, 1)
                    pe.wait_ge(m_evd, f + 1)
                    pe.wait_ge(m_eva, f + 1)
                    for hf in range(2):
                        if t == tl[0]:
                            unit_arrived(pe, ("o", l, hf))
                        w = rview(UI["o", l, hf], 512)
                        for k in range(KT):
                            last = mm(bank(2 + hf), ynT[:, k, :], w[:, k, :], k == 0, k == KT - 1)
                    last.then_inc(op_ps, 1)
                    pe.wait_ge(f_h2, f + 1)
                    for k in range(KT):
                        last = tp(ps[2][:, k * P:(k + 1) * P], hTf[:, t, k * P:(k + 1) * P])
                    last.then_inc(f_tp, 1)
                    pe.wait_ge(f_evd, f + 1)
                    pe.wait_ge(f_eva, f + 1)
                    for k in range(KT):
                        last = mm(bank(7)[:, 0:NG + NE], ynT[:, k, :], wr[:, k, :], k == 0, k == KT - 1)
                    last.then_inc(lg_ps, 1)

                nt = NF[l]
                t0 = full(l)[0]
                pe.wait_ge(r_m, l + 1)
                rk = bank(6)[:, 0:nt * NE].rearrange("p (t e) -> p t e", e=NE)
                mm(rk, cst[:, K_UP:K_UP + P], r_M[:, t0:, :], True, False)
                mm(rk, cst[:, K_ONE:K_ONE + P], r_pre[:, t0:, :], False, True)
                mm(bank(6)[:, T * NE:T * NE + NE], cst[:, K_ONE:K_ONE + P], r_tot).then_inc(r_rank, 1)
                if l == 0:
                    broadcast(l, bcn, ((modc, 40), (modc, 40)), (0, 1))
                else:
                    broadcast(l, bcn, ((modc, 40),), (1,))
                pe.wait_ge(lg_ok, fn(l, T - 1) + 1)
                if l + 1 < DEPTH:
                    modulation(l + 1, 0, 12)

                pe.wait_ge(bc_ok, 8 if l == 0 else 12)

                def rows_tp(i, s):
                    pe.wait_ge(g_in[s], i * 16 + 16 * (in_slot[s] * l + 1))
                    for k in range(KT):
                        last = tp(ps[0][:, k * P:(k + 1) * P], G[s][:, k * P:(k + 1) * P])
                    last.then_inc(g_tp, 1)

                def expert(i, s, more, first=False):
                    e1 = i * 3 + (NE * l + s + 1)
                    pe.wait_ge(g_evd, e1)
                    pe.wait_ge(g_eva, e1)
                    pe.wait_ge(ew_in[s], i * 32 + 32 * (in_slot[s] * l + 1))
                    for k in range(KT):
                        last = mm(bank(2), GT[s][:, k, :], eup(s)[:, k, :], k == 0, k == KT - 1)
                    last.then_inc(e_up, 1)
                    if more:
                        rows_tp(i + (s + 1) // 3, (s + 1) % 3)
                    pe.wait_ge(e_a, e1)
                    for k in range(2):
                        last = tp(bank(3)[:, k * P:(k + 1) * P], av[s][:, k * P:(k + 1) * P])
                    last.then_inc(e_aT, 1)
                    pe.wait_ge(e_aTs, e1)
                    outs_free(i, s, e1)
                    for hf in range(2):
                        for k in range(2):
                            last = mm(bank(4 + hf), aT[s][:, k, :], edn(s)[:, k, hf * 512:(hf + 1) * 512], k == 0, k == 1)
                    last.then_inc(e_dn, 1)

                def outs_free(i, s, e1):
                    pe.wait_ge(e_yd, e1)
                    pe.wait_ge(e_ya, e1)

                rows_tp(0, 0)
                for s in range(3):
                    expert(0, s, True, first=True)
                with pe.Fori(1, (NE - 1) // 3) as i:
                    for s in range(3):
                        expert(i, s, True)
                expert((NE - 1) // 3, 0, False)

                o = ov[l]
                v = nc.tensor.value_load(ctl[0:1, 12:13], min_val=0, max_val=NOV)
                pe.wait_ge(e_yd, NE * (l + 1) + 1)
                pe.wait_ge(e_ya, NE * (l + 1) + 1)
                with pe.If(v > 0):
                    with pe.Fori(0, v) as i:
                        pe.wait_ge(o["g"], i * 16 + 16)
                        for k in range(KT):
                            last = tp(ps[0][:, k * P:(k + 1) * P], G[0][:, k * P:(k + 1) * P])
                        last.then_inc(o["step"], 1)
                        pe.wait_ge(o["step"], i * STEPS + STEP["ev"])
                        pe.wait_ge(o["w"], i * 32 + 32)
                        for k in range(KT):
                            last = mm(bank(2), GT[0][:, k, :], eup(0)[:, k, :], k == 0, k == KT - 1)
                        last.then_inc(o["step"], 1)
                        pe.wait_ge(o["step"], i * STEPS + STEP["a"])
                        for k in range(2):
                            last = tp(bank(3)[:, k * P:(k + 1) * P], av[0][:, k * P:(k + 1) * P])
                        last.then_inc(o["step"], 1)
                        pe.wait_ge(o["step"], i * STEPS + STEP["aTs"])
                        for hf in range(2):
                            for k in range(2):
                                last = mm(bank(4 + hf), aT[0][:, k, :], edn(0)[:, k, hf * 512:(hf + 1) * 512], k == 0, k == 1)
                        last.then_inc(o["step"], 1)


_INS = ['x', 'c', 'ctx', 'c_ctx', 'w_mod', 'b_mod', 'g_attn_norm', 'w_in', 'sgu_v_gain', 'sgu_w', 'sgu_b',
        'conv_w', 'gqa_q_gain', 'gqa_k_gain', 'mla_qa_gain', 'mla_w_qb', 'mla_kva_gain', 'mla_w_kvb',
        'mla_q_gain', 'mla_k_gain', 'g_group_out', 'w_out', 'g_ffn_norm', 'w_router_group',
        'b_router_group', 'w_router_expert', 'b_router_expert', 'w_expert_up', 'w_expert_down']


def kernel(**inputs):
    import numpy as _np
    import concourse.bacc as _bacc
    from concourse import mybir as _mybir
    from concourse.bass_utils import run_bass_kernel_spmd as _run

    nc = _bacc.Bacc("TRN2", target_bir_lowering=False, num_devices=1)
    arrays = {"in_consts": constants()}
    args = [nc.dram_tensor("in_consts", (P, NCONST), _mybir.dt.float32, kind="ExternalInput").ap()]
    for name in _INS:
        a = _np.ascontiguousarray(inputs[name])
        arrays[f"in_{name}"] = a
        args.append(nc.dram_tensor(f"in_{name}", a.shape, _mybir.dt.from_np(a.dtype), kind="ExternalInput").ap())
    args.append(nc.dram_tensor("out_0", (1, SEQ, D), _mybir.dt.float32, kind="ExternalOutput").ap())
    block_kernel(nc, *args)
    r = _run(nc, [arrays], core_ids=[0])
    return r.results[0]["out_0"]
```

```python
import math
from contextlib import ExitStack

import concourse.bass as bass
from concourse import mybir

D = 1024
SEQ = 512
CTX = 256
DEPTH = 2
P = 128
KT = D // P
T = (SEQ + CTX) // P
TC = CTX // P
TOK = T * P
GW = 256
HEADS = 4
HD = 64
KVH = 2
ROPE = 32
DH = HD + ROPE
QLORA = 256
KVLORA = 128
NG = 4
NE = 16
EPG = NE // NG
FE = D // 4
EPS = 1e-6
GRID_W = 64
THETA = 10000.0
IN_COLS = 5 * GW + GW + 2 * 128 + QLORA + KVLORA + ROPE
C_AU, C_BB, C_BC, C_BX = 0, 2 * GW, 3 * GW, 4 * GW
C_CQ = 5 * GW
C_CK = C_CQ + GW
C_DQ = C_CK + 2 * KVH * HD
C_DKV = C_DQ + QLORA
KVC = 2 * KVH * HD + KVLORA + ROPE
UNIT = KT * 512
RING = 5
EXP_SLOTS = 3
EXP_F = KT * 512 + 2 * D
XT = TOK * 2 // P
NOV = XT - 1
ROWS = (NE + NOV + 1) * P
BIG = 1e30

V_BMOD, V_GA, V_GF, V_GO = 0, 48, 56, 64
V_QA, V_KVA, V_SB, V_CW = 72, 74, 75, 79
V_C, V_CC = 85, 93
V_ROWS = 101

K_ID, K_UP, K_ONE = 0, 128, 256
K_RC, K_RS = 384, 384 + 256
K_DC, K_DS = 896, 896 + 128
K_P4, K_P16, K_E, K_15E, K_V = 1152, 1156, 1172, 1188, 1204
K_IN4, K_IQ5, K_I8 = 1216, 1220, 1225
K_H = 1233
K_EPS = 1234
NCONST = 1236


def constants():
    import numpy as np
    c = np.zeros((P, NCONST), np.float32)
    c[:, K_ID:K_ID + P] = np.eye(P)
    c[:, K_UP:K_UP + P] = np.triu(np.ones((P, P)), 1)
    c[:, K_ONE:K_ONE + P] = 1.0
    pos = np.arange(SEQ)
    row, col = (pos // GRID_W).astype(np.float32), (pos % GRID_W).astype(np.float32)
    for width, kc, ks in ((HD, K_RC, K_RS), (ROPE, K_DC, K_DS)):
        nf = width // 4
        inv = np.float32(THETA) ** (-np.arange(nf, dtype=np.float32) / np.float32(nf))
        ang = np.concatenate([row[:, None] * inv, col[:, None] * inv], -1).astype(np.float32)
        cos = np.repeat(np.cos(ang), 2, -1)
        sin = np.repeat(np.sin(ang), 2, -1)
        sin[:, 0::2] *= -1
        c[:, kc:kc + 4 * width] = cos.reshape(4, P, width).transpose(1, 0, 2).reshape(P, -1)
        c[:, ks:ks + 4 * width] = sin.reshape(4, P, width).transpose(1, 0, 2).reshape(P, -1)
    c[:, K_P4:K_P4 + 4] = 4 - np.arange(4)
    c[:, K_P16:K_P16 + 16] = 16 - np.arange(16)
    c[:, K_E:K_E + 16] = np.arange(16)
    c[:, K_15E:K_15E + 16] = NE - 1 - np.arange(16)
    c[:, K_V:K_V + 12] = np.arange(12)
    c[:, K_IN4:K_IN4 + 4] = [1 / HD, 1 / HD, 1 / KVLORA, 1 / ROPE]
    c[:, K_IQ5:K_IQ5 + 5] = [1 / HD] * 4 + [1 / QLORA]
    c[:, K_I8:K_I8 + 8] = [1 / HD] * 4 + [1 / ROPE] * 4
    c[:, K_H] = -0.5
    return c


def block_kernel(nc, consts, x, c, ctx, c_ctx, w_mod, b_mod, g_attn_norm, w_in, sgu_v_gain, sgu_w,
                 sgu_b, conv_w, gqa_q_gain, gqa_k_gain, mla_qa_gain, mla_w_qb, mla_kva_gain,
                 mla_w_kvb, mla_q_gain, mla_k_gain, g_group_out, w_out, g_ffn_norm, w_rg, b_rg,
                 w_re, b_re, w_up, w_down, out):
    F32, I32 = mybir.dt.float32, mybir.dt.int32
    ALU, ACT, AX = mybir.AluOpType, mybir.ActivationFunctionType, mybir.AxisListType
    MUL, ADD, SUB = ALU.mult, ALU.add, ALU.subtract

    LAYERS = range(DEPTH)

    def full(l):
        return range(T) if l < DEPTH - 1 else range(TC, T)

    def an(l, t):
        return T * l + t

    def fn(l, t):
        return an(l, t) - TC * (l == DEPTH - 1)

    FULL = [(l, t) for l in LAYERS for t in full(l)]
    NF = {l: len(full(l)) for l in LAYERS}

    def keys(t):
        return CTX if t < TC else TOK

    NU = 2 * HEADS

    SLOTS = 3 * NU
    AT = dict(conv_tp=0, squares=1, norm=4, tp0=4, tp1=5, out0=6, out1=8, ffn_sq=9, q=9, q_norm=11,
              lora_tp=12, q2=13, q2_norm=14, ffn_tp0=15, ffn_tp1=16, logits=17, qc_tp=19, qd_tp=20)

    units = [("mod", 0, i) for i in range(4)] + [("kv", 0, 0), ("b", 0, 0), ("b", 0, 1), ("a", 0, 0)]
    units += [("mod", 0, i) for i in range(4, 12)] + [("q", 0, 0), ("o", 0, 0), ("o", 0, 1)]
    units += [("mod", 1, i) for i in range(12)]
    L0_UNITS = len(units)
    units += [("kv", 1, 0), ("b", 1, 0), ("b", 1, 1), ("a", 1, 0), ("q", 1, 0), ("o", 1, 0), ("o", 1, 1)]
    UI = {u: n for n, u in enumerate(units)}
    LAST_OF_LAYER = {0: L0_UNITS, 1: len(units)}

    es = ExitStack()
    with es:
        def sb(name, shape, dt=F32):
            return es.enter_context(nc.sbuf_tensor(name, shape, dt))

        def sem(name):
            return es.enter_context(nc.semaphore(name))

        wreg = sb("weights", [P, RING * UNIT])
        xb = sb("x_tile", [P, 2, D])
        hT = sb("h_transposed", [P, T, KT, P])
        kv = sb("keys_values", [P, 6144])
        yB = sb("y_conv", [P, 2, TOK])
        yA = sb("y_sgu", [P, T, GW])
        yn = sb("y_norm", [P, D])
        ynT = sb("y_norm_transposed", [P, KT, P])
        bc = sb("broadcast_rows", [P, 3, D])
        scr = sb("scratch", [P, 4, 784])
        yCDs = sb("y_attention", [P, 2, 2 * GW])
        cst = sb("constants", [P, NCONST])
        wqb = sb("mla_w_qb_s", [P, 2, HEADS * DH])
        wkvb = sb("mla_w_kvb_s", [P, 512])
        wsT = sb("sgu_w_transposed", [P, HEADS, P])
        wr = sb("w_router", [P, KT, NG + NE])
        rows = sb("row_vectors", [P, 600])
        vecT = sb("column_vectors", [P, DEPTH, V_ROWS])
        sT = sb("silu_c", [P, KT, 2])
        modc = sb("modulation", [P, DEPTH, 48, 2])
        a1 = sb("scale1", [P, DEPTH, KT, 2])
        a2 = sb("scale2", [P, DEPTH, KT, 2])
        qCT = sb("q_gqa_T", [P, 2, P])
        qDT = sb("q_mla_T", [P, HEADS, P])
        small = sb("small", [P, 400])
        posi = sb("positions", [P, T, 2], I32)
        ctl = sb("overflow_control", [P, 16], I32)

        kCT = kv[:, 0:768]
        kDT = kv[:, 768:768 + 3072].rearrange("p (h t) -> p h t", h=HEADS)
        vC = kv[:, 3840:3840 + 768].rearrange("p (t n) -> p t n", t=T)
        vD = kv[:, 4608:6144].rearrange("p (t n) -> p t n", t=T)
        G = [kv[:, s * D:(s + 1) * D] for s in range(3)]
        GT = [kv[:, (3 + s) * D:(4 + s) * D].rearrange("p (k n) -> p k n", k=KT) for s in range(3)]
        hTf = hT[:, :, :, :].rearrange("p t k n -> p t (k n)")
        yo = [hTf[:, s, :] for s in range(3)]
        yg = [[hTf[:, 2 * b + a, :] for a in range(2)] for b in range(2)]
        SC = [scr[:, i, :] for i in range(4)]
        scf = scr[:, :, :].rearrange("p a n -> p (a n)")
        zero = SC[3][:, 0:512]

        kSq, k2Sq = SC[0][:, 0:288], SC[0][:, 288:544]
        kCb = [SC[1][:, 0:128], SC[1][:, 128:256]]
        kRb = [SC[1][:, 256:288], SC[1][:, 288:320]]
        kTmp = SC[1][:, 320:576]
        kDb = SC[2][:, 0:HEADS * DH].rearrange("p (h n) -> p h n", h=HEADS)
        kLora, kLoraT = SC[2][:, 384:512], SC[2][:, 512:640]
        cvC, cvZ, cvA = SC[0], SC[1], SC[2]
        gb = [SC[0][:, 0:512], SC[1][:, 0:512]]
        gSq, gMix = SC[2][:, 0:256], SC[2][:, 256:512]
        PB = [SC[0], SC[1]]
        PT = SC[2]
        qC = SC[3][:, 0:256]
        qD = SC[3][:, 256:640].rearrange("p (h n) -> p h n", h=HEADS)
        junk5 = wkvb[:, :]
        junk10 = wkvb[:, :].bitcast(mybir.dt.bfloat16)
        wsf = wsT[:, :, :].rearrange("p h n -> p (h n)")
        lora, qTmp = wsf[:, 0:256], wsf[:, 0:256]
        loraT = wsf[:, 256:512].rearrange("p (k n) -> p k n", k=2)
        sg = [scf[:, s * 256:(s + 1) * 256] for s in range(3)]
        av = [scf[:, (3 + s) * 256:(4 + s) * 256] for s in range(3)]
        aT = [scf[:, (6 + s) * 256:(7 + s) * 256].rearrange("p (k n) -> p k n", k=2) for s in range(3)]
        junk = bc[:, 0, :]

        rpos = [0]

        def rbuf(n):
            rpos[0] += n
            return scf[:, rpos[0] - n:rpos[0]]

        def r3(n):
            return rbuf(T * n).rearrange("p (t n) -> p t n", t=T)

        r_max, r_oh, r_sc, r_dif, r_sum, r_w1 = r3(1), r3(4), r3(4), r3(4), r3(1), r3(1)
        r_L, r_neg, r_t16, r_oh1, r_oh2, r_m1, r_m2 = r3(16), r3(4), r3(16), r3(16), r3(16), r3(1), r3(1)
        r_M, r_pre, r_rank_, r_j, r_row = r3(16), r3(16), r3(16), r3(16), r3(16)
        r_tot, r_cnt, r_nov, r_end, r_ovb, r_one = [rbuf(16) for _ in range(6)]
        r_cmp = rbuf(12 * 16).rearrange("p (v e) -> p v e", v=12)
        r_ctl = rbuf(16)
        r_pf = r3(2)

        nss, nrs = small[:, 0:2], small[:, 2:4]
        kss, krs = [small[:, 4:8], small[:, 8:12]], [small[:, 12:16], small[:, 16:20]]
        k2ss, k2rs = [small[:, 20:24], small[:, 24:28]], [small[:, 28:32], small[:, 32:36]]
        ass, ars = [small[:, 36:40], small[:, 40:44]], [small[:, 44:48], small[:, 48:52]]
        qss, qrs, q2ss, q2rs = small[:, 52:57], small[:, 57:62], small[:, 62:70], small[:, 70:78]
        mss, mrs, fss, frs = small[:, 78:82], small[:, 82:86], small[:, 86:87], small[:, 87:88]
        nmax, esum, rinv = small[:, 88:96], small[:, 96:104], small[:, 104:112]
        logits = small[:, 256:376].rearrange("p (t n) -> p t n", t=T)
        wts = small[:, 376:388].rearrange("p (t a) -> p t a", t=T)

        def ring(n):
            return wreg[:, (n % RING) * UNIT:(n % RING + 1) * UNIT]

        def rview(n, cols):
            return ring(n)[:, 0:KT * cols].rearrange("p (k n) -> p k n", k=KT)

        def eup(s):
            return wreg[:, s * EXP_F:s * EXP_F + KT * 512].rearrange("p (k n) -> p k n", k=KT)

        def edn(s):
            return wreg[:, s * EXP_F + KT * 512:(s + 1) * EXP_F].rearrange("p (k n) -> p k n", k=2)

        ident = cst[:, K_ID:K_ID + P]
        R_SGU, R_CQ, R_CK, R_MQ, R_MK, R_RB = 0, 256, 320, 384, 480, 576

        ps = [es.enter_context(nc.psum_tensor(f"ps{i}", [P, 1024], F32)) for i in range(4)]

        def bank(i):
            return ps[i // 2][:, (i % 2) * 512:(i % 2) * 512 + 512]

        xmid = nc.dram_tensor("x_mid", [DEPTH, TOK, D], F32, kind="Internal").ap()
        xnext = nc.dram_tensor("x_next", [TOK, D], F32, kind="Internal").ap()
        hs = nc.dram_tensor("h_sorted", [ROWS, D], F32, kind="Internal").ap()
        ys = nc.dram_tensor("y_sorted", [ROWS, D], F32, kind="Internal").ap()

        hsv, ysv = [v.rearrange("(e p) d -> e p d", p=P) for v in (hs, ys)]
        N_ZERO = ROWS // P // 4 + (ROWS // P - NE) // 4

        const_in = sem("const_in")
        vec_in = sem("vec_in")
        rowv_in = sem("rowv_in")
        smallw_in = sem("smallw_in")
        vec_tp = sem("vec_tp")
        vec_ok = sem("vec_ok")
        ws_tp = sem("ws_tp")
        ws_ok = sem("ws_ok")
        kvx_in, qx_in, bx_in = sem("kv_unit_tail"), sem("q_unit_tail"), [sem("conv_unit_tail0"), sem("conv_unit_tail1")]
        unit_in = [sem(f"unit_in{i}") for i in range(RING)]
        mod_u = sem("mod_u")
        mod_ok = sem("mod_ok")
        x_in = [sem("x_in0"), sem("x_in1")]
        n_sq, n_rs, n_xn, n_tp, n_evd, n_eva = [sem(f"norm_{s}") for s in ("sq", "rs", "xn", "tp", "evd", "eva")]
        k_ps, k_sq, k_ss, k_rs, k_nrm, k_lT, k_lTs = [sem(f"kv_{s}") for s in ("ps", "sq", "ss", "rs", "nrm", "loraT", "loraTs")]
        k2_ps, k2_sq, k2_ss, k2_rs, k2_nrm, k_all, k_tp, k_tpd, k_tpa = [
            sem(f"kv2_{s}") for s in ("ps", "sq", "ss", "rs", "nrm", "all", "tp", "tpd", "tpa")]
        b_ps, b_c, b_ok = [sem(f"conv_{s}") for s in ("ps", "c", "ok")]
        a_ps, a_gelu, a_ss, a_rs, a_v, a_mix, a_ok = [sem(f"sgu_{s}") for s in ("ps", "gelu", "ss", "rs", "v", "mix", "ok")]
        bc_ps, bc_ok = sem("bc_ps"), sem("bc_ok")
        q_ps, q_sq, q_ss, q_rs, q_lora, q_lT, q_lTs = [sem(f"q_{s}") for s in ("ps", "sq", "ss", "rs", "lora", "loraT", "loraTs")]
        q2_ps, q2_sq, q2_ss, q2_rs, q2_nrm, q_all, q_tp, q_tpd, q_tpa = [
            sem(f"q2_{s}") for s in ("ps", "sq", "ss", "rs", "nrm", "all", "tp", "tpd", "tpa")]
        s_ps, s_mx, s_p, p_tp, p_evd, p_eva, o_ps, o_ok = [
            sem(f"att_{s}") for s in ("scores", "max", "probs", "tp", "evd", "eva", "pv", "out")]
        yb_tp, yb_ok, m_sq, m_rs, m_yn, m_tp, m_evd, m_eva, op_ps, op_ev, x1_ok = [
            sem(f"merge_{s}") for s in ("conv_tp", "conv", "sq", "rs", "yn", "tp", "evd", "eva", "out", "out_read", "x1")]
        f_sq, f_rs, f_h2, f_tp, f_evd, f_eva, lg_ps, lg_ok = [
            sem(f"ffn_{s}") for s in ("sq", "rs", "h2", "tp", "evd", "eva", "logits", "logits_ok")]
        x1_st = sem("x1_stored")
        zero_ok, zero_st = sem("zero_ok"), sem("zero_stored")
        r_exp_in, r_exp, r_m, r_rank, r_pos = [sem(f"route_{s}") for s in ("exp_in", "exp", "mask", "rank", "pos")]
        sc_done = sem("rows_scattered")
        ew_in = [sem(f"expert_w{s}") for s in range(3)]
        g_in = [sem(f"expert_rows{s}") for s in range(3)]
        g_tp, g_evd, g_eva, e_up, e_sg, e_a, e_aT, e_aTs, e_dn, e_yd, e_ya = [
            sem(f"expert_{s}") for s in ("tp", "evd", "eva", "up", "sg", "a", "aT", "aTs", "dn", "yd", "ya")]
        y_st = [sem(f"expert_stored{s}") for s in range(3)]
        STEP = dict(tp=1, ev=3, up=4, sg=5, a=6, aT=7, aTs=8, dn=9, y=11)
        STEPS = 11
        ov = {}
        for l in LAYERS:
            ov[l] = {s: sem(f"ov{l}_{s}") for s in ("w", "g", "step", "st", "end")}
        c_in = [sem("comb_in0"), sem("comb_in1")]
        c_ok, c_st = sem("comb_ok"), sem("comb_stored")
        dve_ch, pool_ch = sem("dve_chain"), sem("pool_chain")

        xuse = {}
        for l in LAYERS:
            for t in range(T):
                xuse["n", l, t] = len(xuse)
            for t in full(l):
                xuse["u", l, t] = len(xuse)
            for t in full(l):
                xuse["c", l, t] = len(xuse)

        in_slot = [(NE - s + 2) // 3 for s in range(3)]

        def x_tile(kind, l, t):
            return xb[:, xuse[kind, l, t] % 2, :]

        def x_arrived(eng, kind, l, t):
            q = xuse[kind, l, t]
            eng.wait_ge(x_in[q % 2], 16 * (q // 2 + 1))

        def unit_arrived(eng, u):
            n = UI[u]
            eng.wait_ge(unit_in[n % RING], 16 * (n // RING + 1))

        def unit_released(eng, n):
            kind, l, i = units[n]
            if kind == "mod":
                eng.wait_ge(mod_u, 12 * l + i + 1)
            elif kind == "kv":
                eng.wait_ge(k_ps, T * (l + 1))
            elif kind == "b":
                eng.wait_ge(b_ps, 2 * l + i + 1)
            elif kind == "a":
                eng.wait_ge(a_ps, fn(l, T - 1) + 1)
            elif kind == "q":
                eng.wait_ge(q_ps, fn(l, T - 1) + 1)
            else:
                eng.wait_ge(op_ps, 2 * fn(l, T - 1) + i + 1)

        def seg(t0, t1):
            return slice(t0 * P, t1 * P)

        ZC, ZL = 1, CTX + 2

        def sides(l):
            tl = [None, None, *full(l), None, None]
            return [(tl[i - 1], tl[i], tl[i + 1]) for i in range(1, len(tl) - 1)]

        block = es.enter_context(nc.Block())

        @block.sync
        def _(sp):
            def load_unit(n):
                kind, l, i = units[n]
                if n >= L0_UNITS and units[n - RING][1] == 0:
                    sp.wait_ge(e_dn, NE)
                    sp.wait_ge(ov[0]["end"], 1)
                elif n >= RING:
                    unit_released(sp, n - RING)
                done = unit_in[n % RING]
                wi = w_in[l].rearrange("(k p) n -> p k n", p=P)
                if kind == "mod":
                    sp.dma_start(rview(n, 512), w_mod[l].rearrange("(k p) n -> p k n", p=P)[:, :, i * 512:(i + 1) * 512]).then_inc(done, 16)
                elif kind == "a":
                    sp.dma_start(rview(n, 512), wi[:, :, C_AU:C_AU + 512]).then_inc(done, 16)
                elif kind == "o":
                    sp.dma_start(rview(n, 512), w_out[l].rearrange("(k p) n -> p k n", p=P)[:, :, i * 512:(i + 1) * 512]).then_inc(done, 16)
                elif kind == "kv":
                    v = rview(n, KVC)
                    sp.dma_start(v[:, :, 0:256], wi[:, :, C_CK:C_CK + 256]).then_inc(done, 16)
                    sp.dma_start(v[:, :, 256:KVC], wi[:, :, C_DKV:C_DKV + KVLORA + ROPE]).then_inc(kvx_in, 16)
                elif kind == "q":
                    v = rview(n, 512)
                    sp.dma_start(v[:, :, 0:256], wi[:, :, C_CQ:C_CQ + 256]).then_inc(done, 16)
                    sp.dma_start(v[:, :, 256:512], wi[:, :, C_DQ:C_DQ + 256]).then_inc(qx_in, 16)
                else:
                    v = rview(n, 384)
                    for c3 in range(3):
                        c0 = C_BB + c3 * GW + i * P
                        sp.dma_start(v[:, :, c3 * P:(c3 + 1) * P], wi[:, :, c0:c0 + P]).then_inc(done if c3 == 0 else bx_in[i], 16)

            def load_x(kind, l, t):
                q = xuse[kind, l, t]
                if kind in "nu":
                    src = (ctx[0, t * P:(t + 1) * P, :] if t < TC else x[0, (t - TC) * P:(t - TC + 1) * P, :]) \
                        if l == 0 else xnext[t * P:(t + 1) * P, :]
                else:
                    src = xmid[l, t * P:(t + 1) * P, :]
                sp.dma_start(xb[:, q % 2, :], src).then_inc(x_in[q % 2], 16)

            def store_x(l, t):
                dst = xnext[t * P:(t + 1) * P, :] if l + 1 < DEPTH else out[0, (t - TC) * P:(t - TC + 1) * P, :]
                sp.dma_start(dst, x_tile("c", l, t)).then_inc(c_st, 16)

            sp.dma_start(cst[:, :], consts).then_inc(const_in, 16)
            for l in LAYERS:
                st = scr[0:P, l, 0:P]
                for r, src, n in ((V_BMOD, b_mod, 48), (V_GA, g_attn_norm, 8), (V_GF, g_ffn_norm, 8),
                                  (V_GO, g_group_out, 8), (V_QA, mla_qa_gain, 2), (V_KVA, mla_kva_gain, 1)):
                    sp.dma_start(st[r:r + n, :], src[l].rearrange("(r n) -> r n", n=P)).then_inc(vec_in, 16)
                sp.dma_start(st[V_SB:V_SB + 4, :], sgu_b[l]).then_inc(vec_in, 16)
                sp.dma_start(st[V_CW:V_CW + 6, :], conv_w[l].rearrange("w (j n) -> (w j) n", n=P)).then_inc(vec_in, 16)
                sp.dma_start(st[V_C:V_C + 8, :], c[0].rearrange("(r n) -> r n", n=P)).then_inc(vec_in, 16)
                sp.dma_start(st[V_CC:V_CC + 8, :], c_ctx.rearrange("(r n) -> r n", n=P)).then_inc(vec_in, 16)

            def load_small(l):
                for o, src, n in ((R_SGU, sgu_v_gain, 256), (R_CQ, gqa_q_gain, 64), (R_CK, gqa_k_gain, 64),
                                  (R_MQ, mla_q_gain, 96), (R_MK, mla_k_gain, 96), (R_RB, b_rg, 4), (R_RB + 4, b_re, 16)):
                    sp.dma_start(rows[:, o:o + n], src[l].rearrange("(a n) -> a n", a=1).to_broadcast([P, n])).then_inc(rowv_in, 16)
                sp.dma_start(wqb[:, :, :], mla_w_qb[l].rearrange("(k p) n -> p k n", p=P)).then_inc(smallw_in, 16)
                sp.dma_start(wkvb[:, :], mla_w_kvb[l]).then_inc(smallw_in, 16)
                sp.dma_start(wr[:, :, 0:NG], w_rg[l].rearrange("(k p) n -> p k n", p=P)).then_inc(smallw_in, 16)
                sp.dma_start(wr[:, :, NG:], w_re[l].rearrange("(k p) n -> p k n", p=P)).then_inc(smallw_in, 16)
                sp.dma_start(ynT[:, 0:HEADS, :], sgu_w[l].rearrange("h i j -> i h j")).then_inc(smallw_in, 16)

            def norm_loads(l, first):
                for t in range(first, T):
                    n = an(l, t)
                    if t >= 2:
                        sp.wait_ge(n_xn, n - 1)
                    load_x("n", l, t)

            load_unit(0)
            load_x("n", 0, 0)
            load_x("n", 0, 1)
            load_small(0)
            for n in range(1, RING):
                load_unit(n)
            norm_loads(0, 2)
            for n in range(RING, UI["mod", 1, 2]):
                load_unit(n)
                if units[n] == ("b", 0, 1):
                    sp.wait_ge(zero_ok, 1)
                    zh, zy = [v.rearrange("(a p b) d -> a p b d", p=P, b=4) for v in (hs, ys)]
                    for dst in [zh[a] for a in range(ROWS // P // 4)] + [zy[a] for a in range(NE // 4, ROWS // P // 4)]:
                        sp.dma_start(dst.rearrange("p b (c n) -> p (b c) n", n=512),
                                     zero.rearrange("p (a n) -> p a n", a=1).to_broadcast([P, 8, 512])).then_inc(zero_st, 16)

            for l in LAYERS:
                if l:
                    sp.wait_ge(c_st, 16 * NF[0])
                    load_x("n", l, 0)
                    load_x("n", l, 1)
                    for n in range(L0_UNITS, L0_UNITS + RING):
                        load_unit(n)
                    norm_loads(l, 2)
                    for n in range(L0_UNITS + RING, len(units)):
                        load_unit(n)
                for t in full(l):
                    f = fn(l, t)
                    if t == full(l)[0]:
                        sp.wait_ge(n_xn, an(l, T - 1) + 1)
                    if t >= full(l)[0] + 2:
                        sp.wait_ge(x1_st, 16 * (f - 1))
                        sp.wait_ge(f_h2, f - 1)
                    load_x("u", l, t)
                    if t > full(l)[0]:
                        sp.wait_ge(x1_ok, f)
                        sp.dma_start(xmid[l, (t - 1) * P:t * P, :], x_tile("u", l, t - 1)).then_inc(x1_st, 16)
                sp.wait_ge(x1_ok, fn(l, T - 1) + 1)
                sp.dma_start(xmid[l, (T - 1) * P:T * P, :], x_tile("u", l, T - 1)).then_inc(x1_st, 16)
                if l == 0:
                    for n in range(UI["mod", 1, 2], L0_UNITS):
                        load_unit(n)

                last = LAST_OF_LAYER[l]

                def load_expert(e, s):
                    sp.dma_start(eup(s), w_up[l, e].rearrange("(k p) n -> p k n", p=P)).then_inc(ew_in[s], 16)
                    sp.dma_start(edn(s), w_down[l, e].rearrange("(k p) n -> p k n", p=P)).then_inc(ew_in[s], 16)

                for s, slots in enumerate(((0, 1), (1, 2), (3, 4))):
                    for r in slots:
                        unit_released(sp, max(n for n in range(last) if n % RING == r))
                    load_expert(s, s)
                sp.wait_ge(sc_done, 16 * 2 * (fn(l, T - 1) + 1))
                for s in range(3):
                    sp.dma_start(G[s], hsv[s]).then_inc(g_in[s], 16)

                def store_y(i, s):
                    sp.wait_ge(e_yd, i * 3 + (NE * l + s + 2))
                    sp.wait_ge(e_ya, i * 3 + (NE * l + s + 2))
                    sp.dma_start(ysv[i * 3 + s], yo[s]).then_inc(y_st[s], 16)

                with sp.Fori(0, (NE - 1) // 3 - 1) as i:
                    for s in range(3):
                        sp.wait_ge(e_dn, i * 3 + (NE * l + s + 1))
                        e = i * 3 + (s + 3)
                        sp.dma_start(G[s], hsv[e]).then_inc(g_in[s], 16)
                        sp.dma_start(eup(s), w_up[l, e].rearrange("(k p) n -> p k n", p=P)).then_inc(ew_in[s], 16)
                        sp.dma_start(edn(s), w_down[l, e].rearrange("(k p) n -> p k n", p=P)).then_inc(ew_in[s], 16)
                        store_y(i, s)
                sp.wait_ge(e_dn, NE * l + NE - 3)
                sp.dma_start(G[0], hsv[NE - 1]).then_inc(g_in[0], 16)
                load_expert(NE - 1, 0)
                for s in range(3):
                    store_y((NE - 1) // 3 - 1, s)
                if l == 0:
                    sp.wait_ge(lg_ok, fn(0, T - 1) + 1)
                    load_small(1)
                store_y((NE - 1) // 3, 0)

                sp.wait_ge(r_pos, l + 1)
                v = nc.sync.value_load(ctl[0:1, 12:13], min_val=0, max_val=NOV)
                o = ov[l]
                for s in range(3):
                    sp.wait_ge(y_st[s], 16 * in_slot[s] * (l + 1))
                sp.sem_inc(o["st"], 16)
                with sp.If(v > 0):
                    with sp.Fori(0, v) as i:
                        e = nc.sync.value_load(ctl[0:1, bass.ds(i, 1)], min_val=0, max_val=NE - 1)
                        sp.wait_ge(o["st"], i * 16 + 16)
                        sp.dma_start(G[0], hsv[i + NE]).then_inc(o["g"], 16)
                        sp.dma_start(eup(0), w_up[l, e].rearrange("(k p) n -> p k n", p=P)).then_inc(o["w"], 16)
                        sp.dma_start(edn(0), w_down[l, e].rearrange("(k p) n -> p k n", p=P)).then_inc(o["w"], 16)
                        sp.wait_ge(o["step"], i * STEPS + STEP["y"])
                        sp.dma_start(ysv[i + NE], yo[0]).then_inc(o["st"], 16)
                sp.wait_ge(o["st"], v * 16 + 16)
                sp.sem_inc(o["end"], 1)

                for t in full(l):
                    f = fn(l, t)
                    if t == full(l)[0]:
                        sp.wait_ge(x1_st, 16 * (fn(l, T - 1) + 1))
                        sp.wait_ge(f_h2, fn(l, T - 1) + 1)
                    if t >= full(l)[0] + 2:
                        sp.wait_ge(c_st, 16 * (f - 1))
                    load_x("c", l, t)
                    if t > full(l)[0]:
                        sp.wait_ge(c_ok, f)
                        store_x(l, t - 1)
                sp.wait_ge(c_ok, fn(l, T - 1) + 1)
                store_x(l, T - 1)
            sp.wait_ge(c_st, 16 * len(FULL))
            sp.wait_ge(zero_st, 16 * N_ZERO)

        @block.gpsimd
        def _(pool):
            chain = [0]

            def link(ins):
                chain[0] += 1
                ins.then_inc(pool_ch, 1)
                pool.wait_ge(pool_ch, chain[0])

            pool.sem_inc(e_yd, 1)
            pool.sem_inc(e_ya, 1)
            pool.memset(zero, 0.0).then_inc(zero_ok, 1)
            half = cst[:, K_H:K_H + 1]

            def rsqrt(out, ss, n, inv):
                if isinstance(inv, float):
                    link(pool.tensor_scalar(ss, ss, inv, EPS, MUL, ADD))
                else:
                    link(pool.tensor_tensor(ss, ss, inv, MUL))
                    link(pool.tensor_scalar(ss, ss, EPS, None, ADD))
                return pool.tensor_tensor(out, ss, half.to_broadcast([P, n]), ALU.pow)

            def rope(x4, heads, width, kc, ks, t, tmp):
                cos = cst[:, kc + (t - TC) * width:kc + (t - TC + 1) * width].rearrange("p (a n) -> p a n", a=1).to_broadcast([P, heads, width])
                sin = cst[:, ks + (t - TC) * width:ks + (t - TC + 1) * width]
                tm = tmp[:, 0:heads * width].rearrange("p (h n b) -> p h n b", h=heads, b=2)
                xs = x4.rearrange("p h (n b) -> p h n b", b=2)
                sv = sin.rearrange("p (n b) -> p n b", b=2)
                for b in range(2):
                    link(pool.tensor_tensor(tm[:, :, :, b], xs[:, :, :, 1 - b],
                                            sv[:, :, b].rearrange("p (a n) -> p a n", a=1).to_broadcast([P, heads, width // 2]), MUL))
                link(pool.tensor_tensor(x4, x4, cos, MUL))
                return pool.tensor_tensor(x4, x4, tmp[:, 0:heads * width].rearrange("p (h n) -> p h n", h=heads), ADD)

            pool.wait_ge(const_in, 16)

            for l in LAYERS:
                lastf = fn(l, T - 1)
                for i in range(T + 3):
                    if i < T:
                        n = an(l, i)
                        pool.wait_ge(n_sq, n + 1)
                        rsqrt(nrs[:, n % 2:n % 2 + 1], nss[:, n % 2:n % 2 + 1], 1, 1.0 / D).then_inc(n_rs, 1)
                    if 0 <= i - 1 < T:
                        n = an(l, i - 1)
                        pool.wait_ge(k_ss, n + 1)
                        rsqrt(krs[n % 2], kss[n % 2], 4, cst[:, K_IN4:K_IN4 + 4]).then_inc(k_rs, 1)
                    if 0 <= i - 2 < T:
                        n = an(l, i - 2)
                        pool.wait_ge(k2_ss, n + 1)
                        rsqrt(k2rs[n % 2], k2ss[n % 2], 4, 1.0 / HD).then_inc(k2_rs, 1)
                    if 0 <= i - 3 < T:
                        t = i - 3
                        n = an(l, t)
                        pool.wait_ge(k2_nrm, n + 1)
                        if t >= TC:
                            link(rope(kCb[n % 2].rearrange("p (h n) -> p h n", h=KVH), KVH, HD, K_RC, K_RS, t, kTmp))
                            link(rope(kRb[n % 2].rearrange("p (h n) -> p h n", h=1), 1, ROPE, K_DC, K_DS, t, kTmp))
                        pool.tensor_copy(kDb[:, :, HD:DH], kRb[n % 2].rearrange("p (a n) -> p a n", a=1).to_broadcast([P, HEADS, ROPE])).then_inc(k_all, 1)
                for t in full(l):
                    f = fn(l, t)
                    pool.wait_ge(a_ss, f + 1)
                    rsqrt(ars[f % 2], ass[f % 2], 4, 1.0 / HD).then_inc(a_rs, 1)
                if l == 0:
                    pool.wait_ge(zero_st, 16 * N_ZERO)

                def side(slot, prev, nxt):
                    if prev is not None:
                        g = fn(l, prev)
                        if slot == AT["squares"]:
                            pool.wait_ge(m_sq, g + 1)
                            rsqrt(mrs, mss, 4, 1.0 / GW).then_inc(m_rs, 1)
                        if slot == AT["ffn_sq"]:
                            pool.wait_ge(f_sq, g + 1)
                            rsqrt(frs, fss, 1, 1.0 / D).then_inc(f_rs, 1)
                    if nxt is not None:
                        f = fn(l, nxt)
                        if slot == AT["q"]:
                            pool.wait_ge(q_ss, f + 1)
                            rsqrt(qrs, qss, 5, cst[:, K_IQ5:K_IQ5 + 5]).then_inc(q_rs, 1)
                        if slot == AT["q2"]:
                            pool.wait_ge(q2_ss, f + 1)
                            rsqrt(q2rs, q2ss, 8, cst[:, K_I8:K_I8 + 8]).then_inc(q2_rs, 1)
                        if slot == AT["q2_norm"]:
                            pool.wait_ge(q2_nrm, f + 1)
                            if nxt >= TC:
                                link(rope(qC.rearrange("p (h n) -> p h n", h=HEADS), HEADS, HD, K_RC, K_RS, nxt, qTmp))
                                rope(qD[:, :, HD:DH], HEADS, ROPE, K_DC, K_DS, nxt, qTmp).then_inc(q_all, 1)
                            else:
                                pool.sem_inc(q_all, 1)

                for prev, t, nxt in sides(l):
                    for slot in range(SLOTS):
                        side(slot, prev, nxt)

                pool.wait_ge(r_pos, l + 1)
                for t in full(l):
                    for a in range(2):
                        pool.indirect_dma_start(out=hs, out_offset=bass.IndirectOffsetOnAxis(ap=posi[:, t, a:a + 1], axis=0),
                                                in_=hTf[:, t, :], in_offset=None).then_inc(sc_done, 16)
                pool.wait_ge(sc_done, 16 * 2 * (lastf + 1))

                for s in range(3):
                    pool.wait_ge(y_st[s], 16 * in_slot[s] * (l + 1))
                pool.wait_ge(ov[l]["end"], 1)

                for t in full(l):
                    f = fn(l, t)
                    if t >= full(l)[0] + 2:
                        pool.wait_ge(c_ok, f - 1)
                    for a in range(2):
                        pool.indirect_dma_start(out=yg[f % 2][a], out_offset=None, in_=ys,
                                                in_offset=bass.IndirectOffsetOnAxis(ap=posi[:, t, a:a + 1], axis=0)).then_inc(c_in[f % 2], 16)

        @block.scalar
        def _(act):
            def copy(out, in_):
                return act.activation(out, in_, ACT.Copy)

            act.wait_ge(vec_tp, 1)
            for l in LAYERS:
                copy(vecT[:, l, :], bank(6 + l)[:, 0:V_ROWS])
            act.activation(sT[:, :, 0], bank(6)[:, V_CC:V_CC + KT], ACT.Silu)
            act.activation(sT[:, :, 1], bank(6)[:, V_C:V_C + KT], ACT.Silu).then_inc(vec_ok, 1)

            for l in LAYERS:
                act.wait_ge(ws_tp, l + 1)
                copy(wsT[:, :, :], bank(0).rearrange("p (h n) -> p h n", h=HEADS)).then_inc(ws_ok, 1)
                for i in range(T + 3):
                    if i < T:
                        n = an(l, i)
                        x_arrived(act, "n", l, i)
                        if n >= 2:
                            act.wait_ge(n_rs, n - 1)
                        act.activation(junk, x_tile("n", l, i), ACT.Square,
                                       accum_out=nss[:, n % 2:n % 2 + 1]).then_inc(n_sq, 1)
                    if 0 <= i - 1 < T:
                        n = an(l, i - 1)
                        kps = bank(4 + n % 2)
                        act.wait_ge(k_ps, n + 1)
                        copy(vC[:, i - 1, :], kps[:, 128:256])
                        act.wait_ge(k_ss, n)
                        act.activation(kSq[:, 0:128], kps[:, 0:128], ACT.Square)
                        act.activation(kSq[:, 128:288], kps[:, 256:416], ACT.Square).then_inc(k_sq, 1)
                    if 0 <= i - 2 < T:
                        n = an(l, i - 2)
                        act.wait_ge(k_lT, n + 1)
                        act.wait_ge(k2_ps, n)
                        act.activation(kLoraT, bank(6)[:, 0:P], ACT.Copy,
                                       scale=vecT[:, l, V_KVA:V_KVA + 1]).then_inc(k_lTs, 1)
                        k2 = bank(7).rearrange("p (h n) -> p h n", h=HEADS)
                        act.wait_ge(k2_ps, n + 1)
                        copy(vD[:, i - 2, :].rearrange("p (h n) -> p h n", h=HEADS), k2[:, :, HD:2 * HD])
                        act.wait_ge(k2_ss, n)
                        act.activation(k2Sq.rearrange("p (h n) -> p h n", h=HEADS), k2[:, :, 0:HD], ACT.Square).then_inc(k2_sq, 1)
                    if 0 <= i - 3 < T:
                        n = an(l, i - 3)
                        act.wait_ge(k_tp, n + 1)
                        copy(kCT[:, (i - 3) * P:(i - 2) * P], bank(2)[:, 0:P]).then_inc(k_tpa, 1)
                    if i < T:
                        n = an(l, i)
                        s = int(i >= TC)
                        act.wait_ge(n_tp, n + 1)
                        act.wait_ge(mod_ok, 2 * l + 1)
                        for k in range(4, KT):
                            last = act.activation(hT[:, i, k, :], ps[0][:, k * P:(k + 1) * P], ACT.Identity,
                                                  bias=modc[:, l, k, s:s + 1], scale=a1[:, l, k, s:s + 1])
                        last.then_inc(n_eva, 1)
                for j in range(2):
                    b = 2 * l + j
                    act.wait_ge(b_ps, b + 1)
                    act.wait_ge(b_ok, b)
                    if l == 0:
                        copy(cvC[:, 0:CTX], bank(3)[:, 0:CTX])
                    copy(cvC[:, CTX:TOK], bank(2)).then_inc(b_c, 1)
                for t in full(l):
                    f = fn(l, t)
                    act.wait_ge(a_ps, f + 1)
                    if f >= 2:
                        act.wait_ge(a_ok, f - 1)
                    act.activation(gb[f % 2], bank(6 + f % 2), ACT.Gelu_apprx_tanh).then_inc(a_gelu, 1)

                def broadcast_evac(b0, n, s0):
                    for v in range(n):
                        act.wait_ge(bc_ps, b0 + v + 1)
                        copy(bc[:, s0 + v, :], ps[1 + v % 2][:, :]).then_inc(bc_ok, 1)

                def side(slot, prev, nxt):
                    if prev is not None:
                        g = fn(l, prev)
                        if slot == AT["squares"]:
                            act.wait_ge(yb_ok, g + 1)
                            act.wait_ge(o_ok, NU * (g + 1))
                            y = yCDs[:, g % 2, :]
                            for j, src in enumerate((yA[:, prev, :], yn[:, GW:2 * GW], y[:, 0:GW], y[:, GW:])):
                                last = act.activation(junk10[:, j * GW:(j + 1) * GW], src, ACT.Square, accum_out=mss[:, j:j + 1])
                            last.then_inc(m_sq, 1)
                        if slot == AT["tp1"]:
                            act.wait_ge(m_tp, 2 * g + 2)
                            for k in range(4, KT):
                                last = act.activation(ynT[:, k, :], bank(7)[:, (k - 4) * P:(k - 3) * P], ACT.Copy,
                                                      scale=vecT[:, l, V_GO + k:V_GO + k + 1])
                            last.then_inc(m_eva, 1)
                        if slot == AT["ffn_sq"]:
                            act.wait_ge(x1_ok, g + 1)
                            act.wait_ge(m_sq, g + 1)
                            act.activation(junk10, x_tile("u", l, prev), ACT.Square, accum_out=fss).then_inc(f_sq, 1)
                        if slot == AT["ffn_tp1"]:
                            act.wait_ge(f_tp, 2 * g + 2)
                            copy(ynT[:, 4:, :], bank(7).rearrange("p (k n) -> p k n", k=4)).then_inc(f_eva, 1)
                    if nxt is not None:
                        f = fn(l, nxt)
                        if slot == AT["q"]:
                            act.wait_ge(q_ps, f + 1)
                            if prev is not None:
                                act.wait_ge(f_sq, fn(l, prev) + 1)
                            act.activation(junk5, bank(7), ACT.Square).then_inc(q_sq, 1)
                        if slot == AT["lora_tp"]:
                            act.wait_ge(q_lT, f + 1)
                            for k in range(2):
                                last = act.activation(loraT[:, k, :], bank(7)[:, k * P:(k + 1) * P], ACT.Copy,
                                                      scale=vecT[:, l, V_QA + k:V_QA + k + 1])
                            last.then_inc(q_lTs, 1)
                        if slot == AT["q2"]:
                            act.wait_ge(q2_ps, f + 1)
                            act.activation(junk5[:, 0:HEADS * DH], bank(7)[:, 0:HEADS * DH], ACT.Square).then_inc(q2_sq, 1)
                        if slot == AT["qc_tp"]:
                            act.wait_ge(q_tp, 2 * f + 1)
                            copy(qCT[:, :, :], bank(7)[:, 0:256].rearrange("p (g n) -> p g n", g=2)).then_inc(q_tpa, 1)

                bcn = 8 * l
                broadcast_evac(bcn, 3, 0)
                for prev, t, nxt in sides(l):
                    if t is not None:
                        f = fn(l, t)
                        nk = keys(t)

                        def exp(u):
                            w = NU * f + u
                            act.wait_ge(s_mx, w + 1)
                            if w >= 2:
                                act.wait_ge(p_tp, w - 1)
                            act.activation(PB[u % 2][:, 0:nk], ps[u % 2][:, 0:nk], ACT.Exp, bias=nmax[:, u:u + 1],
                                           accum_out=esum[:, u:u + 1]).then_inc(s_p, 1)

                        exp(0)
                    for slot in range(SLOTS):
                        if t is not None:
                            u, part = divmod(slot, 3)
                            if part == 0 and u + 1 < NU:
                                exp(u + 1)
                            if part == 1:
                                w = NU * f + u
                                act.wait_ge(p_tp, w + 1)
                                act.wait_ge(o_ps, w)
                                copy(PT[:, nk // 2:nk], bank(5)[:, 0:nk // 2]).then_inc(p_eva, 1)
                        side(slot, prev, nxt)
                    if l == 0 and t == TC:
                        broadcast_evac(bcn + 3, 3, 0)
                bcn += 6 if l == 0 else 3

                t0 = full(l)[0]
                act.wait_ge(r_exp_in, 2 * l + 1)
                act.activation(r_dif[:, t0:, :], r_dif[:, t0:, :], ACT.Exp).then_inc(r_exp, 1)
                act.wait_ge(r_exp_in, 2 * l + 2)
                act.activation(r_m2[:, t0:, :], r_m2[:, t0:, :], ACT.Exp).then_inc(r_exp, 1)
                if l == 0:
                    broadcast_evac(bcn, 2, 0)
                else:
                    broadcast_evac(bcn, 1, 1)

                def rows_evac(count, s):
                    act.wait_ge(g_tp, count)
                    copy(GT[s][:, 4:, :], ps[0][:, 512:].rearrange("p (k n) -> p k n", k=4)).then_inc(g_eva, 1)

                def expert(i, s, more, first=False):
                    e1 = i * 3 + (NE * l + s + 1)
                    act.wait_ge(e_up, e1)
                    act.activation(sg[s], bank(2)[:, 0:FE], ACT.Silu).then_inc(e_sg, 1)
                    if more:
                        rows_evac(e1 + 1, (s + 1) % 3)
                    act.wait_ge(e_aT, e1)
                    copy(aT[s], bank(3)[:, 0:FE].rearrange("p (k n) -> p k n", k=2)).then_inc(e_aTs, 1)
                    act.wait_ge(e_dn, e1)
                    if l or not first:
                        act.wait_ge(y_st[s], i * 16 + 16 * in_slot[s] * l)
                    copy(yo[s][:, 512:], bank(5)).then_inc(e_ya, 1)

                rows_evac(NE * l + 1, 0)
                for s in range(3):
                    expert(0, s, True, first=True)
                with act.Fori(1, (NE - 1) // 3) as i:
                    for s in range(3):
                        expert(i, s, True)
                expert((NE - 1) // 3, 0, False)

                o = ov[l]
                v = nc.scalar.value_load(ctl[0:1, 12:13], min_val=0, max_val=NOV)
                with act.If(v > 0):
                    with act.Fori(0, v) as i:
                        act.wait_ge(o["step"], i * STEPS + STEP["tp"])
                        copy(GT[0][:, 4:, :], ps[0][:, 512:].rearrange("p (k n) -> p k n", k=4)).then_inc(o["step"], 1)
                        act.wait_ge(o["step"], i * STEPS + STEP["up"])
                        act.activation(sg[0], bank(2)[:, 0:FE], ACT.Silu).then_inc(o["step"], 1)
                        act.wait_ge(o["step"], i * STEPS + STEP["aT"])
                        copy(aT[0], bank(3)[:, 0:FE].rearrange("p (k n) -> p k n", k=2)).then_inc(o["step"], 1)
                        act.wait_ge(o["step"], i * STEPS + STEP["dn"])
                        copy(yo[0][:, 512:], bank(5)).then_inc(o["step"], 1)

        @block.vector
        def _(dve):
            chain = [0]

            def link(ins):
                chain[0] += 1
                ins.then_inc(dve_ch, 1)
                dve.wait_ge(dve_ch, chain[0])

            def tt(out, a, b, op):
                return dve.tensor_tensor(out, a, b, op)

            def ts(out, a, s1, s2, op0, op1=None):
                return dve.tensor_scalar(out, a, s1, s2, op0) if op1 is None else dve.tensor_scalar(out, a, s1, s2, op0, op1)

            def each(v, n):
                return v.rearrange("p (h a) -> p h a", a=1).to_broadcast([P, v.shape[1], n])

            def over(v, h):
                return v.rearrange("p (a n) -> p a n", a=1).to_broadcast([P, h, v.shape[1]])

            def heads(v, h):
                return v.rearrange("p (h n) -> p h n", h=h)

            def total(out, in_):
                return dve.tensor_reduce(out, in_, AX.X, ADD)

            def modulation(l, half):
                c0, c1 = (0, 16) if half == 0 else (16, 48)
                dve.wait_ge(mod_u, 4 if (l, half) == (0, 0) else 12 * (l + 1))
                m = bank(7)[:, 2 * c0:2 * c1].rearrange("p (c s) -> p c s", s=2)
                link(tt(modc[:, l, c0:c1, :], m, each(vecT[:, l, V_BMOD + c0:V_BMOD + c1], 2), ADD))
                dst, sc, g = (a1, 8, V_GA) if half == 0 else (a2, 32, V_GF)
                link(ts(dst[:, l, :, :], modc[:, l, sc:sc + KT, :], 1.0, None, ADD))
                tt(dst[:, l, :, :], dst[:, l, :, :], each(vecT[:, l, g:g + KT], 2), MUL).then_inc(mod_ok, 1)

            dve.wait_ge(vec_ok, 1)
            modulation(0, 0)
            for l in LAYERS:
                dve.wait_ge(rowv_in, 16 * 7 * (l + 1))
                ts(rows[:, R_CQ:R_CQ + HD], rows[:, R_CQ:R_CQ + HD], HD ** -0.5, None, MUL)
                link(ts(rows[:, R_MQ:R_MQ + DH], rows[:, R_MQ:R_MQ + DH], DH ** -0.5, None, MUL))
                dve.wait_ge(mod_ok, 2 * l + 1)
                for i in range(T + 3):
                    if i < T:
                        n = an(l, i)
                        s = int(i >= TC)
                        dve.wait_ge(n_rs, n + 1)
                        dve.wait_ge(n_tp, n)
                        ts(yn[:, :], x_tile("n", l, i), nrs[:, n % 2:n % 2 + 1], None, MUL).then_inc(n_xn, 1)
                        dve.wait_ge(n_tp, n + 1)
                        for k in range(4):
                            last = ts(hT[:, i, k, :], ps[0][:, k * P:(k + 1) * P],
                                      a1[:, l, k, s:s + 1], modc[:, l, k, s:s + 1], MUL, ADD)
                        last.then_inc(n_evd, 1)
                    if 0 <= i - 1 < T:
                        n = an(l, i - 1)
                        dve.wait_ge(k_sq, n + 1)
                        total(kss[n % 2][:, 0:2], heads(kSq[:, 0:128], 2))
                        total(kss[n % 2][:, 2:3], kSq[:, 128:256])
                        total(kss[n % 2][:, 3:4], kSq[:, 256:288]).then_inc(k_ss, 1)
                    if 0 <= i - 3 < T:
                        n = an(l, i - 3)
                        dve.wait_ge(k2_rs, n + 1)
                        dve.wait_ge(k_tp, n)
                        link(tt(kDb[:, :, 0:HD], heads(bank(7), HEADS)[:, :, 0:HD], each(k2rs[n % 2], HD), MUL))
                        tt(kDb[:, :, 0:HD], kDb[:, :, 0:HD], over(rows[:, R_MK:R_MK + HD], HEADS), MUL).then_inc(k2_nrm, 1)
                    if 0 <= i - 2 < T:
                        n = an(l, i - 2)
                        kps, r, kc = bank(4 + n % 2), krs[n % 2], heads(kCb[n % 2], 2)
                        dve.wait_ge(k_rs, n + 1)
                        dve.wait_ge(k_lT, n)
                        if n >= 2:
                            dve.wait_ge(k_tp, n - 1)
                        ts(kLora, kps[:, 256:384], r[:, 2:3], None, MUL)
                        link(tt(kc, heads(kps[:, 0:128], 2), each(r[:, 0:2], HD), MUL))
                        tt(kc, kc, over(rows[:, R_CK:R_CK + HD], 2), MUL)
                        dve.scalar_tensor_tensor(kRb[n % 2], kps[:, 384:416], r[:, 3:4],
                                                 rows[:, R_MK + HD:R_MK + DH], MUL, MUL).then_inc(k_nrm, 1)
                        dve.wait_ge(k2_sq, n + 1)
                        total(k2ss[n % 2], heads(k2Sq, HEADS)).then_inc(k2_ss, 1)
                    if 0 <= i - 3 < T:
                        n = an(l, i - 3)
                        dve.wait_ge(k_tp, n + 1)
                        dve.tensor_copy(kDT[0:DH, :, (i - 3) * P:(i - 2) * P], heads(bank(3), HEADS)[0:DH]).then_inc(k_tpd, 1)

                lo, zl = (0, ZC) if l == 0 else (CTX, ZL)
                if l == 0:
                    width = TOK + 1
                else:
                    width = SEQ
                for j in range(2):
                    b = 2 * l + j
                    wc = [vecT[:, l, V_CW + 2 * w + j:V_CW + 2 * w + j + 1] for w in range(3)]
                    dve.wait_ge(b_c, b + 1)
                    for z in (0, ZL - 1, ZL + SEQ):
                        dve.memset(cvZ[:, z:z + 1], 0.0)
                    if l == 0:
                        tt(cvZ[:, ZC:ZC + CTX], cvC[:, 0:CTX], bank(5)[:, 0:CTX], MUL)
                    link(tt(cvZ[:, ZL:ZL + SEQ], cvC[:, CTX:TOK], bank(4), MUL))
                    link(ts(cvA[:, 0:width], cvZ[:, zl - 1:zl - 1 + width], wc[0], None, MUL))
                    link(dve.scalar_tensor_tensor(cvA[:, 0:width], cvZ[:, zl:zl + width], wc[1], cvA[:, 0:width], MUL, ADD))
                    link(dve.scalar_tensor_tensor(cvA[:, 0:width], cvZ[:, zl + 1:zl + 1 + width], wc[2], cvA[:, 0:width], MUL, ADD))
                    if l == 0:
                        tt(yB[:, j, 0:CTX], cvA[:, 0:CTX], bank(1)[:, 0:CTX], MUL)
                    tt(yB[:, j, CTX:TOK], cvA[:, ZL - zl:ZL - zl + SEQ], bank(0), MUL).then_inc(b_ok, 1)

                tl = list(full(l))
                for i in range(len(tl) + 1):
                    if i < len(tl):
                        f = fn(l, tl[i])
                        dve.wait_ge(a_gelu, f + 1)
                        dve.wait_ge(a_ss, f)
                        link(tt(gSq, gb[f % 2][:, GW:], gb[f % 2][:, GW:], MUL))
                        total(ass[f % 2], heads(gSq, HEADS)).then_inc(a_ss, 1)
                    if i:
                        t = tl[i - 1]
                        f = fn(l, t)
                        v = heads(gb[f % 2][:, GW:], HEADS)
                        dve.wait_ge(a_rs, f + 1)
                        link(tt(v, v, each(ars[f % 2], HD), MUL))
                        tt(v, v, heads(rows[:, R_SGU:R_SGU + GW], HEADS), MUL).then_inc(a_v, 1)
                        dve.wait_ge(a_mix, f + 1)
                        link(tt(heads(gMix, HEADS), heads(bank(4 + f % 2)[:, 0:GW], HEADS), each(vecT[:, l, V_SB:V_SB + 4], HD), ADD))
                        tt(yA[:, t, :], gMix, gb[f % 2][:, 0:GW], MUL).then_inc(a_ok, 1)

                if l == 0:
                    modulation(0, 1)
                def side(slot, prev, nxt):
                    if prev is not None:
                        g = fn(l, prev)
                        xt = x_tile("u", l, prev)
                        h2 = hTf[:, prev, :]
                        if slot == AT["conv_tp"]:
                            dve.wait_ge(yb_tp, g + 1)
                            if g:
                                dve.wait_ge(x1_ok, g)
                            dve.tensor_copy(yn[:, GW:2 * GW], bank(7)[:, 0:GW]).then_inc(yb_ok, 1)
                        if slot == AT["norm"]:
                            dve.wait_ge(m_rs, g + 1)
                            y = yCDs[:, g % 2, :]
                            for j, src in enumerate((yA[:, prev, :], yn[:, GW:2 * GW], y[:, 0:GW], y[:, GW:])):
                                last = ts(yn[:, j * GW:(j + 1) * GW], src, mrs[:, j:j + 1], None, MUL)
                            last.then_inc(m_yn, 1)
                        if slot == AT["tp0"]:
                            dve.wait_ge(m_tp, 2 * g + 1)
                            for k in range(4):
                                last = ts(ynT[:, k, :], bank(7)[:, k * P:(k + 1) * P], vecT[:, l, V_GO + k:V_GO + k + 1], None, MUL)
                            last.then_inc(m_evd, 1)
                        for hf in range(2):
                            if slot == AT[f"out{hf}"]:
                                if hf == 0:
                                    dve.wait_ge(bc_ok, 3 if prev < TC else 6 if l == 0 else 11)
                                    x_arrived(dve, "u", l, prev)
                                    dve.wait_ge(m_tp, 2 * g + 2)
                                dve.wait_ge(op_ps, 2 * g + hf + 1)
                                c = slice(hf * 512, hf * 512 + 512)
                                tt(yn[:, c], bank(7), bc[:, 2, c], MUL).then_inc(op_ev, 1)
                                dve.wait_ge(op_ev, 2 * g + hf + 1)
                                last = tt(xt[:, c], xt[:, c], yn[:, c], ADD)
                                if hf:
                                    last.then_inc(x1_ok, 1)
                        if slot == AT["ffn_sq"]:
                            dve.wait_ge(f_rs, g + 1)
                            link(dve.scalar_tensor_tensor(h2, xt, frs, bc[:, 0, :], MUL, MUL))
                            tt(h2, h2, bc[:, 1, :], ADD).then_inc(f_h2, 1)
                        if slot == AT["ffn_tp0"]:
                            dve.wait_ge(f_tp, 2 * g + 1)
                            dve.tensor_copy(ynT[:, 0:4, :], bank(7).rearrange("p (k n) -> p k n", k=4)).then_inc(f_evd, 1)
                        if slot == AT["logits"]:
                            dve.wait_ge(lg_ps, g + 1)
                            tt(logits[:, prev, :], bank(7)[:, 0:NG + NE], rows[:, R_RB:R_RB + NG + NE], ADD).then_inc(lg_ok, 1)
                    if nxt is not None:
                        f = fn(l, nxt)
                        q = bank(7)
                        if slot == AT["q"]:
                            dve.wait_ge(q_sq, f + 1)
                            total(qss[:, 0:4], heads(junk5[:, 0:256], HEADS))
                            total(qss[:, 4:5], junk5[:, 256:512]).then_inc(q_ss, 1)
                        if slot == AT["q_norm"]:
                            dve.wait_ge(q_rs, f + 1)
                            ts(lora, q[:, 256:512], qrs[:, 4:5], None, MUL)
                            tt(qC.rearrange("p (g v n) -> p v g n", g=2, v=2), q[:, 0:256].rearrange("p (v g n) -> p v g n", g=2, v=2),
                               qrs[:, 0:4].rearrange("p (v g a) -> p v g a", v=2, a=1).to_broadcast([P, 2, 2, HD]), MUL).then_inc(q_lora, 1)
                            dve.wait_ge(q_lora, f + 1)
                            link(tt(heads(qC, HEADS), heads(qC, HEADS), over(rows[:, R_CQ:R_CQ + HD], HEADS), MUL))
                        if slot == AT["q2"]:
                            dve.wait_ge(q2_sq, f + 1)
                            sq = heads(junk5[:, 0:HEADS * DH], HEADS)
                            total(q2ss[:, 0:4], sq[:, :, 0:HD])
                            total(q2ss[:, 4:8], sq[:, :, HD:DH]).then_inc(q2_ss, 1)
                        if slot == AT["q2_norm"]:
                            dve.wait_ge(q2_rs, f + 1)
                            q2 = heads(q[:, 0:HEADS * DH], HEADS)
                            tt(qD[:, :, 0:HD], q2[:, :, 0:HD], each(q2rs[:, 0:4], HD), MUL)
                            link(tt(qD[:, :, HD:DH], q2[:, :, HD:DH], each(q2rs[:, 4:8], ROPE), MUL))
                            tt(qD, qD, over(rows[:, R_MQ:R_MQ + DH], HEADS), MUL).then_inc(q2_nrm, 1)
                        if slot == AT["qd_tp"]:
                            dve.wait_ge(q_tp, 2 * f + 2)
                            dve.tensor_copy(qDT[0:DH, :, :], heads(bank(7), HEADS)[0:DH]).then_inc(q_tpd, 1)

                for prev, t, nxt in sides(l):
                    if t is not None:
                        f = fn(l, t)
                        nk = keys(t)
                        yt = yCDs[:, f % 2, :]

                        def row_max(u):
                            w = NU * f + u
                            dve.wait_ge(s_ps, w + 1)
                            dve.tensor_reduce(nmax[:, u:u + 1], ps[u % 2][:, 0:nk], AX.X, ALU.max, negate=True).then_inc(s_mx, 1)

                        def head_out(u):
                            w = NU * f + u
                            dve.wait_ge(o_ps, w + 1)
                            link(dve.reciprocal(rinv[:, u:u + 1], esum[:, u:u + 1]))
                            ts(yt[:, u * HD:(u + 1) * HD], bank(6)[:, 0:HD], rinv[:, u:u + 1], None, MUL).then_inc(o_ok, 1)

                        row_max(0)
                    for slot in range(SLOTS):
                        if t is not None:
                            u, part = divmod(slot, 3)
                            if part == 0:
                                if u + 1 < NU:
                                    row_max(u + 1)
                                if u:
                                    head_out(u - 1)
                            if part == 1:
                                w = NU * f + u
                                dve.wait_ge(p_tp, w + 1)
                                dve.tensor_copy(PT[:, 0:nk // 2], bank(4)[:, 0:nk // 2]).then_inc(p_evd, 1)
                        side(slot, prev, nxt)
                    if t is not None:
                        head_out(NU - 1)

                t0 = full(l)[0]
                nt = NF[l]
                U = slice(t0, T)

                def rv(v):
                    return v[:, U, :]

                def along(v, n):
                    return rv(v).to_broadcast([P, nt, n])

                def row(c0, n):
                    return cst[:, c0:c0 + n].rearrange("p (a n) -> p a n", a=1).to_broadcast([P, nt, n])

                def first_max(oh, vals, best, scr_, pref, n):
                    link(dve.tensor_reduce(rv(best), vals, AX.X, ALU.max))
                    link(tt(rv(scr_), vals, along(best, n), ALU.is_ge))
                    link(tt(rv(scr_), rv(scr_), row(pref, n), MUL))
                    link(dve.tensor_reduce(rv(r_sum), rv(scr_), AX.X, ALU.max))
                    link(tt(rv(oh), rv(scr_), along(r_sum, n), ALU.is_equal))

                lg = logits[:, U, :]
                dve.wait_ge(lg_ok, fn(l, T - 1) + 1)
                first_max(r_oh, lg[:, :, 0:NG], r_max, r_sc, K_P4, NG)
                tt(rv(r_dif), lg[:, :, 0:NG], along(r_max, NG), SUB).then_inc(r_exp_in, 1)
                link(ts(rv(r_neg), rv(r_oh), BIG, -BIG, MUL, ADD))
                for t in full(l):
                    last = tt(heads(r_L[:, t, :], NG), heads(logits[:, t, NG:], NG), each(r_neg[:, t, :], EPG), ADD)
                link(last)
                first_max(r_oh1, rv(r_L), r_m1, r_t16, K_P16, NE)
                link(ts(rv(r_t16), rv(r_oh1), -4 * BIG, None, MUL))
                link(tt(rv(r_L), rv(r_L), rv(r_t16), ADD))
                first_max(r_oh2, rv(r_L), r_m2, r_t16, K_P16, NE)
                tt(rv(r_m2), rv(r_m2), rv(r_m1), SUB).then_inc(r_exp_in, 1)
                dve.memset(r_pre[:, t0, :], 0.0)
                link(tt(rv(r_M), rv(r_oh1), rv(r_oh2), ADD))
                for t in range(t0 + 1, T):
                    link(tt(r_pre[:, t, :], r_pre[:, t - 1, :], r_M[:, t - 1, :], ADD))
                tt(r_tot, r_pre[:, T - 1, :], r_M[:, T - 1, :], ADD).then_inc(r_m, 1)
                dve.wait_ge(r_exp, 2 * l + 2)
                link(dve.tensor_reduce(rv(r_sum), rv(r_dif), AX.X, ADD))
                link(ts(rv(r_w1), rv(r_m2), 1.0, None, ADD))
                link(tt(rv(r_w1), rv(r_w1), rv(r_sum), MUL))
                link(dve.reciprocal(wts[:, U, 0:1], rv(r_w1)))
                link(tt(wts[:, U, 1:2], wts[:, U, 0:1], rv(r_m2), MUL))
                dve.wait_ge(r_rank, l + 1)
                dve.tensor_copy(rv(r_rank_), bank(6)[:, 0:nt * NE].rearrange("p (t e) -> p t e", e=NE))
                link(dve.tensor_copy(r_cnt, bank(6)[:, T * NE:T * NE + NE]))
                link(ts(r_nov, r_cnt, float(P), None, ALU.is_gt))
                link(ts(rv(r_j), rv(r_rank_), float(P), None, ALU.is_ge))
                for m in range(2, T):
                    link(dve.scalar_tensor_tensor(rv(r_j), rv(r_rank_), float(m * P), rv(r_j), ALU.is_ge, ADD))
                    link(dve.scalar_tensor_tensor(r_nov, r_cnt, float(m * P), r_nov, ALU.is_gt, ADD))
                link(dve.memset(r_one, 1.0))
                link(dve.tensor_tensor_scan(r_end, r_one, r_nov, 0.0, MUL, ADD))
                link(tt(r_ovb, r_end, r_nov, SUB))
                link(tt(r_ovb, r_ovb, cst[:, K_15E:K_15E + NE], ADD))
                link(tt(rv(r_t16), rv(r_j), over(r_ovb, nt), ADD))
                link(ts(rv(r_row), rv(r_j), 0.0, None, ALU.is_gt))
                link(tt(rv(r_t16), rv(r_t16), rv(r_row), MUL))
                link(tt(rv(r_t16), rv(r_t16), row(K_E, NE), ADD))
                link(tt(rv(r_t16), rv(r_t16), rv(r_j), SUB))
                link(dve.scalar_tensor_tensor(rv(r_row), rv(r_t16), float(P), rv(r_rank_), MUL, ADD))
                for a, oh in enumerate((r_oh1, r_oh2)):
                    link(tt(rv(r_t16), rv(oh), rv(r_row), MUL))
                    link(total(r_pf[:, U, a:a + 1], rv(r_t16)))
                dve.tensor_copy(posi[:, U, :], rv(r_pf))
                link(tt(r_cmp, over(r_end, 12), each(cst[:, K_V:K_V + 12], NE), ALU.is_le))
                link(total(r_ctl[:, 0:12], r_cmp))
                link(ts(r_ctl[:, 0:12], r_ctl[:, 0:12], float(NE - 1), None, ALU.min))
                link(dve.tensor_copy(r_ctl[:, 12:13], r_end[:, NE - 1:NE]))
                dve.tensor_copy(ctl[:, 0:13], r_ctl[:, 0:13]).then_inc(r_pos, 1)

                if l + 1 < DEPTH:
                    modulation(l + 1, 0)
                    modulation(l + 1, 1)

                def rows_evac(count, s):
                    dve.wait_ge(g_tp, count)
                    dve.tensor_copy(GT[s][:, 0:4, :], ps[0][:, 0:512].rearrange("p (k n) -> p k n", k=4)).then_inc(g_evd, 1)

                def expert(i, s, more, first=False):
                    e1 = i * 3 + (NE * l + s + 1)
                    dve.wait_ge(e_sg, e1)
                    tt(av[s], sg[s], bank(2)[:, FE:2 * FE], MUL).then_inc(e_a, 1)
                    if more:
                        rows_evac(e1 + 1, (s + 1) % 3)
                    dve.wait_ge(e_dn, e1)
                    if l or not first:
                        dve.wait_ge(y_st[s], i * 16 + 16 * in_slot[s] * l)
                    dve.tensor_copy(yo[s][:, 0:512], bank(4)).then_inc(e_yd, 1)

                rows_evac(NE * l + 1, 0)
                for s in range(3):
                    expert(0, s, True, first=True)
                with dve.Fori(1, (NE - 1) // 3) as i:
                    for s in range(3):
                        expert(i, s, True)
                expert((NE - 1) // 3, 0, False)

                o = ov[l]
                v = nc.vector.value_load(ctl[0:1, 12:13], min_val=0, max_val=NOV)
                with dve.If(v > 0):
                    with dve.Fori(0, v) as i:
                        dve.wait_ge(o["step"], i * STEPS + STEP["tp"])
                        dve.tensor_copy(GT[0][:, 0:4, :], ps[0][:, 0:512].rearrange("p (k n) -> p k n", k=4)).then_inc(o["step"], 1)
                        dve.wait_ge(o["step"], i * STEPS + STEP["sg"])
                        tt(av[0], sg[0], bank(2)[:, FE:2 * FE], MUL).then_inc(o["step"], 1)
                        dve.wait_ge(o["step"], i * STEPS + STEP["dn"])
                        dve.tensor_copy(yo[0][:, 0:512], bank(4)).then_inc(o["step"], 1)

                for t in full(l):
                    f = fn(l, t)
                    y1, y2 = yg[f % 2]
                    dve.wait_ge(c_in[f % 2], 32 * (f // 2 + 1))
                    if t == t0:
                        dve.wait_ge(bc_ok, 8 if l == 0 else 12)
                    link(ts(y1, y1, wts[:, t, 0:1], None, MUL))
                    link(dve.scalar_tensor_tensor(y1, y2, wts[:, t, 1:2], y1, MUL, ADD))
                    link(tt(y1, y1, bc[:, int(t >= TC), :], MUL))
                    x_arrived(dve, "c", l, t)
                    xt = x_tile("c", l, t)
                    tt(xt, xt, y1, ADD).then_inc(c_ok, 1)

        @block.tensor
        def _(pe):
            def mm(out, lhsT, rhs, start=True, stop=True):
                return pe.matmul(out, lhsT, rhs, start=start, stop=stop)

            def tp(out, in_, n=P):
                return pe.transpose(out, in_, ident[0:n, 0:n])

            def modulation(l, i0, i1):
                for i in range(i0, i1):
                    n = UI["mod", l, i]
                    unit_arrived(pe, ("mod", l, i))
                    w = rview(n, 512)
                    for c4 in range(4):
                        cc = 4 * i + c4
                        for k in range(KT):
                            last = mm(bank(7)[:, 2 * cc:2 * cc + 2], w[:, k, c4 * P:(c4 + 1) * P], sT[:, k, :], k == 0, k == KT - 1)
                    last.then_inc(mod_u, 1)

            def broadcast(l, b0, vecs, s_of):
                for v, (src, c0) in enumerate(vecs):
                    pe.wait_ge(bc_ok, b0 + v - 1) if b0 + v >= 2 else None
                    s = s_of[v]
                    for k in range(KT):
                        last = mm(ps[1 + v % 2][:, k * P:(k + 1) * P], src[:, l, c0 + k, s:s + 1].to_broadcast([P, P]), ident)
                    last.then_inc(bc_ps, 1)

            pe.wait_ge(const_in, 16)
            pe.wait_ge(vec_in, 16 * 10 * DEPTH)
            for l in LAYERS:
                last = tp(bank(6 + l)[:, 0:V_ROWS], scr[0:V_ROWS, l, 0:P], V_ROWS)
            last.then_inc(vec_tp, 1)
            pe.wait_ge(vec_ok, 1)
            modulation(0, 0, 4)

            for l in LAYERS:
                pe.wait_ge(smallw_in, 16 * 5 * (l + 1))
                for h in range(HEADS):
                    last = tp(bank(0)[:, h * P:(h + 1) * P], ynT[:, h, :])
                last.then_inc(ws_tp, 1)
                pe.wait_ge(ws_ok, l + 1)
                ukv = UI["kv", l, 0]
                for i in range(T + 3):
                    if i < T:
                        n = an(l, i)
                        pe.wait_ge(n_xn, n + 1)
                        pe.wait_ge(n_evd, n)
                        pe.wait_ge(n_eva, n)
                        for k in range(KT):
                            last = tp(ps[0][:, k * P:(k + 1) * P], yn[:, k * P:(k + 1) * P])
                        last.then_inc(n_tp, 1)
                    if 0 <= i - 1 < T:
                        n = an(l, i - 1)
                        pe.wait_ge(n_evd, n + 1)
                        pe.wait_ge(n_eva, n + 1)
                        if i == 1:
                            unit_arrived(pe, ("kv", l, 0))
                            pe.wait_ge(kvx_in, 16 * (l + 1))
                        if n >= 2:
                            pe.wait_ge(k_nrm, n - 1)
                        for k in range(KT):
                            last = mm(bank(4 + n % 2)[:, 0:KVC], hT[:, i - 1, k, :], rview(ukv, KVC)[:, k, :], k == 0, k == KT - 1)
                        last.then_inc(k_ps, 1)
                    if 0 <= i - 2 < T:
                        n = an(l, i - 2)
                        pe.wait_ge(k_nrm, n + 1)
                        pe.wait_ge(k_lTs, n)
                        tp(bank(6)[:, 0:P], kLora).then_inc(k_lT, 1)
                        pe.wait_ge(k_lTs, n + 1)
                        pe.wait_ge(k2_nrm, n)
                        if n == 0:
                            pe.wait_ge(mod_ok, 1)
                        mm(bank(7), kLoraT, wkvb[:, :]).then_inc(k2_ps, 1)
                    if 0 <= i - 3 < T:
                        n = an(l, i - 3)
                        pe.wait_ge(k_all, n + 1)
                        pe.wait_ge(k_tpa, n)
                        pe.wait_ge(k_tpd, n)
                        tp(bank(2)[:, 0:P], kCb[n % 2])
                        for h in range(HEADS):
                            last = tp(bank(3)[0:DH, h * P:(h + 1) * P], kDb[:, h, :])
                        last.then_inc(k_tp, 1)

                pe.wait_ge(k_tpa, T * (l + 1))
                pe.wait_ge(k_tpd, T * (l + 1))
                for j in range(2):
                    unit_arrived(pe, ("b", l, j))
                    pe.wait_ge(bx_in[j], 32 * (l + 1))
                    pe.wait_ge(b_ok, 2 * l + j)
                    w = rview(UI["b", l, j], 384)
                    for c3 in range(3):
                        for k in range(KT):
                            last = mm(bank(2 * c3).rearrange("p (t n) -> p t n", n=P), w[:, k, c3 * P:(c3 + 1) * P], hT[:, TC:T, k, :], k == 0, k == KT - 1)
                        if l == 0:
                            for k in range(KT):
                                last = mm(bank(2 * c3 + 1)[:, 0:CTX].rearrange("p (t n) -> p t n", n=P), w[:, k, c3 * P:(c3 + 1) * P], hT[:, 0:TC, k, :], k == 0, k == KT - 1)
                    last.then_inc(b_ps, 1)

                pe.wait_ge(b_ok, 2 * (l + 1))
                unit_arrived(pe, ("a", l, 0))
                w = rview(UI["a", l, 0], 512)
                tl = list(full(l))
                for i in range(len(tl) + 1):
                    if i < len(tl):
                        f = fn(l, tl[i])
                        if f >= 2:
                            pe.wait_ge(a_gelu, f - 1)
                        for k in range(KT):
                            last = mm(bank(6 + f % 2), hT[:, tl[i], k, :], w[:, k, :], k == 0, k == KT - 1)
                        last.then_inc(a_ps, 1)
                    if i:
                        f = fn(l, tl[i - 1])
                        pe.wait_ge(a_v, f + 1)
                        if f >= 2:
                            pe.wait_ge(a_ok, f - 1)
                        for h in range(HEADS):
                            last = mm(bank(4 + f % 2)[:, h * HD:(h + 1) * HD], wsT[:, h, :], gb[f % 2][:, GW + h * HD:GW + (h + 1) * HD])
                        last.then_inc(a_mix, 1)

                pe.wait_ge(a_ok, fn(l, T - 1) + 1)
                if l == 0:
                    pe.wait_ge(a_gelu, fn(l, T - 1) + 1)
                    modulation(0, 4, 12)
                pe.wait_ge(mod_ok, 2 * (l + 1))
                def side(slot, prev, nxt):
                    if prev is not None:
                        g = fn(l, prev)
                        if slot == AT["conv_tp"]:
                            pe.wait_ge(q_tpd, fn(l, T - 1 if nxt is None else nxt - 1) + 1)
                            for j in range(2):
                                last = tp(bank(7)[:, j * P:(j + 1) * P], yB[:, j, prev * P:(prev + 1) * P])
                            last.then_inc(yb_tp, 1)
                        if slot == AT["tp0"]:
                            pe.wait_ge(m_yn, g + 1)
                            for k in range(4):
                                last = tp(bank(7)[:, k * P:(k + 1) * P], yn[:, k * P:(k + 1) * P])
                            last.then_inc(m_tp, 1)
                        if slot == AT["tp1"]:
                            pe.wait_ge(m_evd, g + 1)
                            for k in range(4, KT):
                                last = tp(bank(7)[:, (k - 4) * P:(k - 3) * P], yn[:, k * P:(k + 1) * P])
                            last.then_inc(m_tp, 1)
                        for hf in range(2):
                            if slot == AT[f"out{hf}"]:
                                pe.wait_ge(m_eva, g + 1)
                                if hf:
                                    pe.wait_ge(op_ev, 2 * g + 1)
                                if prev == tl[0]:
                                    unit_arrived(pe, ("o", l, hf))
                                w = rview(UI["o", l, hf], 512)
                                for k in range(KT):
                                    last = mm(bank(7), ynT[:, k, :], w[:, k, :], k == 0, k == KT - 1)
                                last.then_inc(op_ps, 1)
                        if slot == AT["ffn_tp0"]:
                            pe.wait_ge(f_h2, g + 1)
                            if nxt is not None:
                                pe.wait_ge(q2_nrm, fn(l, nxt) + 1)
                            for k in range(4):
                                last = tp(bank(7)[:, k * P:(k + 1) * P], hTf[:, prev, k * P:(k + 1) * P])
                            last.then_inc(f_tp, 1)
                        if slot == AT["ffn_tp1"]:
                            pe.wait_ge(f_evd, g + 1)
                            for k in range(4, KT):
                                last = tp(bank(7)[:, (k - 4) * P:(k - 3) * P], hTf[:, prev, k * P:(k + 1) * P])
                            last.then_inc(f_tp, 1)
                        if slot == AT["logits"]:
                            pe.wait_ge(f_eva, g + 1)
                            for k in range(KT):
                                last = mm(bank(7)[:, 0:NG + NE], ynT[:, k, :], wr[:, k, :], k == 0, k == KT - 1)
                            last.then_inc(lg_ps, 1)
                    if nxt is not None:
                        f = fn(l, nxt)
                        if slot == AT["q"]:
                            if prev is not None:
                                pe.wait_ge(op_ev, 2 * fn(l, prev) + 2)
                            elif f > fn(l, tl[0]):
                                pe.wait_ge(q_tpd, f)
                            else:
                                unit_arrived(pe, ("q", l, 0))
                                pe.wait_ge(qx_in, 16 * (l + 1))
                            w = rview(UI["q", l, 0], 512)
                            for k in range(KT):
                                last = mm(bank(7), hT[:, nxt, k, :], w[:, k, :], k == 0, k == KT - 1)
                            last.then_inc(q_ps, 1)
                        if slot == AT["lora_tp"]:
                            pe.wait_ge(q_lora, f + 1)
                            for k in range(2):
                                last = tp(bank(7)[:, k * P:(k + 1) * P], lora[:, k * P:(k + 1) * P])
                            last.then_inc(q_lT, 1)
                        if slot == AT["q2"]:
                            pe.wait_ge(q_lTs, f + 1)
                            for k in range(2):
                                last = mm(bank(7)[:, 0:HEADS * DH], loraT[:, k, :], wqb[:, k, :], k == 0, k == 1)
                            last.then_inc(q2_ps, 1)
                        if slot == AT["qc_tp"]:
                            pe.wait_ge(q_all, f + 1)
                            if prev is not None:
                                pe.wait_ge(lg_ok, fn(l, prev) + 1)
                            for g2 in range(2):
                                last = tp(bank(7)[:, g2 * P:(g2 + 1) * P], qC[:, g2 * P:(g2 + 1) * P])
                            last.then_inc(q_tp, 1)
                        if slot == AT["qd_tp"]:
                            pe.wait_ge(q_tpa, f + 1)
                            for h in range(HEADS):
                                last = tp(bank(7)[0:DH, h * P:(h + 1) * P], qD[:, h, :])
                            last.then_inc(q_tp, 1)

                bcn = 8 * l
                s = int(l > 0)
                broadcast(l, bcn, ((a2, 0), (modc, 24), (modc, 16)), (s, s, s))
                pe.wait_ge(bc_ok, bcn + 3)
                for prev, t, nxt in sides(l):
                    if t is not None:
                        f = fn(l, t)
                        nk = keys(t)
                        pe.wait_ge(q_tpa, f + 1)
                        pe.wait_ge(q_tpd, f + 1)

                        def scores(u):
                            w = NU * f + u
                            if w >= 2:
                                pe.wait_ge(s_p, w - 1)
                            if u < HEADS:
                                v, g2 = u // 2, u % 2
                                q, kk = qCT[v * HD:(v + 1) * HD, g2, :], kCT[v * HD:(v + 1) * HD, :]
                            else:
                                q, kk = qDT[0:DH, u - HEADS, :], kDT[0:DH, u - HEADS, :]
                            for c0 in range(0, nk, 512):
                                c1 = min(c0 + 512, nk)
                                last = mm(ps[u % 2][:, c0:c1], q, kk[:, c0:c1])
                            last.then_inc(s_ps, 1)

                        scores(0)
                    for slot in range(SLOTS):
                        if t is not None:
                            u, part = divmod(slot, 3)
                            w = NU * f + u
                            if part == 0 and u + 1 < NU:
                                scores(u + 1)
                            if part == 1:
                                pe.wait_ge(s_p, w + 1)
                                pe.wait_ge(p_evd, w)
                                pe.wait_ge(p_eva, w)
                                for k in range(nk // P):
                                    hf, kk = divmod(k, nk // P // 2)
                                    last = tp(bank(4 + hf)[:, kk * P:(kk + 1) * P], PB[u % 2][:, k * P:(k + 1) * P])
                                last.then_inc(p_tp, 1)
                            if part == 2:
                                pe.wait_ge(p_evd, w + 1)
                                pe.wait_ge(p_eva, w + 1)
                                pe.wait_ge(o_ok, w)
                                for k in range(nk // P):
                                    vv = vC[:, k, (u // 2) * HD:(u // 2 + 1) * HD] if u < HEADS else vD[:, k, (u - HEADS) * HD:(u - HEADS + 1) * HD]
                                    last = mm(bank(6)[:, 0:HD], PT[:, k * P:(k + 1) * P], vv, k == 0, k == nk // P - 1)
                                last.then_inc(o_ps, 1)
                        side(slot, prev, nxt)
                    if l == 0 and t == TC:
                        pe.wait_ge(f_h2, fn(l, t - 1) + 1)
                        pe.wait_ge(s_p, NU * (fn(l, t) + 1))
                        pe.wait_ge(p_evd, NU * (fn(l, t) + 1))
                        pe.wait_ge(p_eva, NU * (fn(l, t) + 1))
                        broadcast(l, bcn + 3, ((a2, 0), (modc, 24), (modc, 16)), (1, 1, 1))
                        pe.wait_ge(bc_ok, bcn + 6)
                bcn += 6 if l == 0 else 3

                nt = NF[l]
                t0 = full(l)[0]
                pe.wait_ge(r_m, l + 1)
                rk = bank(6)[:, 0:nt * NE].rearrange("p (t e) -> p t e", e=NE)
                mm(rk, cst[:, K_UP:K_UP + P], r_M[:, t0:, :], True, False)
                mm(rk, cst[:, K_ONE:K_ONE + P], r_pre[:, t0:, :], False, True)
                mm(bank(6)[:, T * NE:T * NE + NE], cst[:, K_ONE:K_ONE + P], r_tot).then_inc(r_rank, 1)
                if l == 0:
                    broadcast(l, bcn, ((modc, 40), (modc, 40)), (0, 1))
                else:
                    broadcast(l, bcn, ((modc, 40),), (1,))
                pe.wait_ge(lg_ok, fn(l, T - 1) + 1)
                if l + 1 < DEPTH:
                    modulation(l + 1, 0, 12)

                pe.wait_ge(bc_ok, 8 if l == 0 else 12)

                def rows_tp(i, s):
                    pe.wait_ge(g_in[s], i * 16 + 16 * (in_slot[s] * l + 1))
                    for k in range(KT):
                        last = tp(ps[0][:, k * P:(k + 1) * P], G[s][:, k * P:(k + 1) * P])
                    last.then_inc(g_tp, 1)

                def expert(i, s, more, first=False):
                    e1 = i * 3 + (NE * l + s + 1)
                    pe.wait_ge(g_evd, e1)
                    pe.wait_ge(g_eva, e1)
                    pe.wait_ge(ew_in[s], i * 32 + 32 * (in_slot[s] * l + 1))
                    for k in range(KT):
                        last = mm(bank(2), GT[s][:, k, :], eup(s)[:, k, :], k == 0, k == KT - 1)
                    last.then_inc(e_up, 1)
                    if more:
                        rows_tp(i + (s + 1) // 3, (s + 1) % 3)
                    pe.wait_ge(e_a, e1)
                    for k in range(2):
                        last = tp(bank(3)[:, k * P:(k + 1) * P], av[s][:, k * P:(k + 1) * P])
                    last.then_inc(e_aT, 1)
                    pe.wait_ge(e_aTs, e1)
                    outs_free(i, s, e1)
                    for hf in range(2):
                        for k in range(2):
                            last = mm(bank(4 + hf), aT[s][:, k, :], edn(s)[:, k, hf * 512:(hf + 1) * 512], k == 0, k == 1)
                    last.then_inc(e_dn, 1)

                def outs_free(i, s, e1):
                    pe.wait_ge(e_yd, e1)
                    pe.wait_ge(e_ya, e1)

                rows_tp(0, 0)
                for s in range(3):
                    expert(0, s, True, first=True)
                with pe.Fori(1, (NE - 1) // 3) as i:
                    for s in range(3):
                        expert(i, s, True)
                expert((NE - 1) // 3, 0, False)

                o = ov[l]
                v = nc.tensor.value_load(ctl[0:1, 12:13], min_val=0, max_val=NOV)
                pe.wait_ge(e_yd, NE * (l + 1) + 1)
                pe.wait_ge(e_ya, NE * (l + 1) + 1)
                with pe.If(v > 0):
                    with pe.Fori(0, v) as i:
                        pe.wait_ge(o["g"], i * 16 + 16)
                        for k in range(KT):
                            last = tp(ps[0][:, k * P:(k + 1) * P], G[0][:, k * P:(k + 1) * P])
                        last.then_inc(o["step"], 1)
                        pe.wait_ge(o["step"], i * STEPS + STEP["ev"])
                        pe.wait_ge(o["w"], i * 32 + 32)
                        for k in range(KT):
                            last = mm(bank(2), GT[0][:, k, :], eup(0)[:, k, :], k == 0, k == KT - 1)
                        last.then_inc(o["step"], 1)
                        pe.wait_ge(o["step"], i * STEPS + STEP["a"])
                        for k in range(2):
                            last = tp(bank(3)[:, k * P:(k + 1) * P], av[0][:, k * P:(k + 1) * P])
                        last.then_inc(o["step"], 1)
                        pe.wait_ge(o["step"], i * STEPS + STEP["aTs"])
                        for hf in range(2):
                            for k in range(2):
                                last = mm(bank(4 + hf), aT[0][:, k, :], edn(0)[:, k, hf * 512:(hf + 1) * 512], k == 0, k == 1)
                        last.then_inc(o["step"], 1)


_INS = ['x', 'c', 'ctx', 'c_ctx', 'w_mod', 'b_mod', 'g_attn_norm', 'w_in', 'sgu_v_gain', 'sgu_w', 'sgu_b',
        'conv_w', 'gqa_q_gain', 'gqa_k_gain', 'mla_qa_gain', 'mla_w_qb', 'mla_kva_gain', 'mla_w_kvb',
        'mla_q_gain', 'mla_k_gain', 'g_group_out', 'w_out', 'g_ffn_norm', 'w_router_group',
        'b_router_group', 'w_router_expert', 'b_router_expert', 'w_expert_up', 'w_expert_down']


def kernel(**inputs):
    import numpy as _np
    import concourse.bacc as _bacc
    from concourse import mybir as _mybir
    from concourse.bass_utils import run_bass_kernel_spmd as _run

    nc = _bacc.Bacc("TRN2", target_bir_lowering=False, num_devices=1)
    arrays = {"in_consts": constants()}
    args = [nc.dram_tensor("in_consts", (P, NCONST), _mybir.dt.float32, kind="ExternalInput").ap()]
    for name in _INS:
        a = _np.ascontiguousarray(inputs[name])
        arrays[f"in_{name}"] = a
        args.append(nc.dram_tensor(f"in_{name}", a.shape, _mybir.dt.from_np(a.dtype), kind="ExternalInput").ap())
    args.append(nc.dram_tensor("out_0", (1, SEQ, D), _mybir.dt.float32, kind="ExternalOutput").ap())
    block_kernel(nc, *args)
    r = _run(nc, [arrays], core_ids=[0])
    return r.results[0]["out_0"]
```
